# Optimizing a Trainium2 kernel written in Bass

```python
import math
import jax, jax.numpy as jnp
from jax import lax
import numpy as np

D_MODEL = 1024
BATCH = 1
SEQ = 256
DEPTH = 2

CHUNK = 64
N_MIXERS = 2
NORM_EPS = 1e-6
ATTN_HEADS = 16
ATTN_KV_HEADS = 4
ATTN_HEAD_DIM = 64
ATTN_GROUP = ATTN_HEADS // ATTN_KV_HEADS
ATTN_WINDOW = 128
WINDOW_CHUNKS = ATTN_WINDOW // CHUNK
ROPE_THETA = 10000.0
ATTN_IN_DIM = (ATTN_HEADS + 2 * ATTN_KV_HEADS) * ATTN_HEAD_DIM
HGRN_HEADS = 8
HGRN_KEY_DIM = D_MODEL // HGRN_HEADS
HGRN_VAL_DIM = D_MODEL // HGRN_HEADS
HGRN_IN_DIM = 4 * D_MODEL
PEER_HEADS = 8
PEER_N_KEYS = 128
PEER_N_EXPERTS = PEER_N_KEYS * PEER_N_KEYS
PEER_TOPK = 16
PEER_QUERY_DIM = 256
PEER_HALF = PEER_QUERY_DIM // 2
PEER_BLOCK = 128

N_ATTN_LAYERS = (DEPTH + N_MIXERS - 1) // N_MIXERS
N_HGRN_LAYERS = DEPTH // N_MIXERS

kernel_name = "hybrid_swa_hgrn2_peer_trunk"

def rmsnorm(x, gain):
    xf = x.astype(jnp.float32)
    y = xf * lax.rsqrt(jnp.mean(xf * xf, axis=-1, keepdims=True) + NORM_EPS)
    return (y * gain.astype(jnp.float32)).astype(x.dtype)

def rope_tables(seq):
    pos = jnp.arange(seq, dtype=jnp.float32)
    inv_freq = ROPE_THETA ** (-jnp.arange(0, ATTN_HEAD_DIM, 2, dtype=jnp.float32) / ATTN_HEAD_DIM)
    ang = pos[:, None] * inv_freq[None, :]
    return jnp.cos(ang)[None, :, None, :], jnp.sin(ang)[None, :, None, :]

def apply_rope(t, cos, sin):
    t1, t2 = jnp.split(t, 2, axis=-1)
    return jnp.concatenate([t1 * cos - t2 * sin, t2 * cos + t1 * sin], axis=-1)

def swa_attention(xn, w_in, sinks, w_out):
    B, S, _ = xn.shape
    nC = S // CHUNK
    qkv = xn @ w_in
    q, k, v = jnp.split(qkv, [ATTN_HEADS * ATTN_HEAD_DIM, (ATTN_HEADS + ATTN_KV_HEADS) * ATTN_HEAD_DIM], axis=-1)
    cos, sin = rope_tables(S)
    q = apply_rope(q.reshape(B, S, ATTN_HEADS, ATTN_HEAD_DIM).astype(jnp.float32), cos, sin)
    k = apply_rope(k.reshape(B, S, ATTN_KV_HEADS, ATTN_HEAD_DIM).astype(jnp.float32), cos, sin)
    v = v.reshape(B, S, ATTN_KV_HEADS, ATTN_HEAD_DIM).astype(jnp.float32)
    qc = q.reshape(B, nC, CHUNK, ATTN_KV_HEADS, ATTN_GROUP, ATTN_HEAD_DIM)
    kc = k.reshape(B, nC, CHUNK, ATTN_KV_HEADS, ATTN_HEAD_DIM)
    vc = v.reshape(B, nC, CHUNK, ATTN_KV_HEADS, ATTN_HEAD_DIM)

    def shift(t, j):
        return jnp.pad(t, ((0, 0), (j, 0), (0, 0), (0, 0), (0, 0)))[:, :nC]

    offsets = list(range(WINDOW_CHUNKS - 1, -1, -1))
    k_band = jnp.concatenate([shift(kc, j) for j in offsets], axis=2)
    v_band = jnp.concatenate([shift(vc, j) for j in offsets], axis=2)
    chunk_idx = jnp.arange(nC)[:, None]
    valid = jnp.concatenate([jnp.broadcast_to(chunk_idx >= j, (nC, CHUNK)) for j in offsets], axis=1)

    scores = jnp.einsum('bcqkgd,bcskd->bckgqs', qc, k_band) * (ATTN_HEAD_DIM ** -0.5)
    scores = jnp.where(valid[None, :, None, None, None, :], scores, -jnp.inf)
    sink = sinks.astype(jnp.float32).reshape(1, 1, ATTN_KV_HEADS, ATTN_GROUP, 1, 1)
    m = jnp.maximum(jnp.max(scores, axis=-1, keepdims=True), sink)
    p = jnp.exp(scores - m)
    probs = p / (jnp.sum(p, axis=-1, keepdims=True) + jnp.exp(sink - m))
    out = jnp.einsum('bckgqs,bcskd->bcqkgd', probs, v_band).reshape(B, S, ATTN_HEADS * ATTN_HEAD_DIM)
    return out.astype(xn.dtype) @ w_out

def hgrn2(xn, w_in, lower_bound, out_gain, w_out):
    B, S, _ = xn.shape
    nC = S // CHUNK
    q, f, i, g = jnp.split(xn @ w_in, 4, axis=-1)
    q = jax.nn.silu(q.astype(jnp.float32))
    gate = lower_bound + (1.0 - lower_bound) * jax.nn.sigmoid(f.astype(jnp.float32))
    log_f = jnp.log(gate)
    k = 1.0 - gate
    iv = i.astype(jnp.float32)

    def to_chunks(t, d):
        return t.reshape(B, nC, CHUNK, HGRN_HEADS, d).transpose(1, 0, 3, 2, 4)

    qs = to_chunks(q, HGRN_KEY_DIM)
    ks = to_chunks(k, HGRN_KEY_DIM)
    vs = to_chunks(iv, HGRN_VAL_DIM)
    bs = jnp.cumsum(to_chunks(log_f, HGRN_KEY_DIM), axis=-2)
    causal = jnp.tril(jnp.ones((CHUNK, CHUNK), dtype=bool))

    def step(state, inp):
        qc, kc, vc, bc = inp
        diff = bc[:, :, :, None, :] - bc[:, :, None, :, :]
        decay = jnp.exp(jnp.where(causal[:, :, None], diff, -jnp.inf))
        scores = jnp.einsum('bhtd,bhsd,bhtsd->bhts', qc, kc, decay)
        o = jnp.einsum('bhts,bhse->bhte', scores, vc) + jnp.einsum('bhtd,bhde->bhte', qc * jnp.exp(bc), state)
        b_last = bc[:, :, -1:, :]
        state = jnp.exp(b_last)[:, :, 0, :, None] * state + jnp.einsum('bhsd,bhse->bhde', kc * jnp.exp(b_last - bc), vc)
        return state, o

    state0 = jnp.zeros((B, HGRN_HEADS, HGRN_KEY_DIM, HGRN_VAL_DIM), jnp.float32)
    _, o = lax.scan(step, state0, (qs, ks, vs, bs))
    o = o.transpose(1, 0, 3, 2, 4).reshape(B, S, HGRN_HEADS, HGRN_VAL_DIM)
    o = rmsnorm(o, out_gain) * jax.nn.silu(g.astype(jnp.float32)).reshape(B, S, HGRN_HEADS, HGRN_VAL_DIM)
    return o.reshape(B, S, D_MODEL).astype(xn.dtype) @ w_out

def peer_ffn(xn, w_q, sub_keys, u_tab, v_tab):
    B, S, D = xn.shape
    xb_all = xn.reshape(-1, PEER_BLOCK, D)
    keys_f = sub_keys.astype(jnp.float32)

    def block(xb):
        q = (xb @ w_q).reshape(PEER_BLOCK, PEER_HEADS, 2, PEER_HALF).astype(jnp.float32)
        s = jnp.einsum('phcd,hckd->phck', q, keys_f)
        sv, si = lax.top_k(s, PEER_TOPK)
        cand = sv[:, :, 0, :, None] + sv[:, :, 1, None, :]
        cv, ci = lax.top_k(cand.reshape(PEER_BLOCK, PEER_HEADS, PEER_TOPK * PEER_TOPK), PEER_TOPK)
        i1 = jnp.take_along_axis(si[:, :, 0], ci // PEER_TOPK, axis=-1)
        i2 = jnp.take_along_axis(si[:, :, 1], ci % PEER_TOPK, axis=-1)
        expert = i1 * PEER_N_KEYS + i2
        gates = jax.nn.softmax(cv, axis=-1)
        u = u_tab[expert]
        act = jax.nn.gelu(jnp.einsum('pd,phkd->phk', xb, u).astype(jnp.float32), approximate=False)
        return jnp.einsum('phk,phkd->pd', (gates * act).astype(xb.dtype), v_tab[expert])

    return lax.map(block, xb_all).reshape(B, S, D)

def setup_inputs(seed: int = 0) -> dict:
    key = jax.random.key(seed)
    ks = jax.random.split(key, 16)
    f32 = jnp.float32
    nrm = lambda k, shape, scale: jax.random.normal(k, shape, f32) * scale
    return {
        'x': nrm(ks[0], (BATCH, SEQ, D_MODEL), 1.0),
        'mixer_norm': 1.0 + nrm(ks[1], (DEPTH, D_MODEL), 0.01),
        'attn_w_in': nrm(ks[2], (N_ATTN_LAYERS, D_MODEL, ATTN_IN_DIM), D_MODEL ** -0.5),
        'attn_sinks': nrm(ks[3], (N_ATTN_LAYERS, ATTN_HEADS), 0.5),
        'attn_w_out': nrm(ks[4], (N_ATTN_LAYERS, ATTN_HEADS * ATTN_HEAD_DIM, D_MODEL), (ATTN_HEADS * ATTN_HEAD_DIM) ** -0.5),
        'hgrn_w_in': nrm(ks[5], (N_HGRN_LAYERS, D_MODEL, HGRN_IN_DIM), D_MODEL ** -0.5),
        'hgrn_lb_raw': nrm(ks[6], (N_HGRN_LAYERS, HGRN_HEADS * HGRN_KEY_DIM), 0.5),
        'hgrn_out_norm': 1.0 + nrm(ks[7], (N_HGRN_LAYERS, HGRN_VAL_DIM), 0.01),
        'hgrn_w_out': nrm(ks[8], (N_HGRN_LAYERS, D_MODEL, D_MODEL), D_MODEL ** -0.5),
        'ffn_norm': 1.0 + nrm(ks[9], (DEPTH, D_MODEL), 0.01),
        'peer_w_q': nrm(ks[10], (DEPTH, D_MODEL, PEER_HEADS * PEER_QUERY_DIM), D_MODEL ** -0.5),
        'peer_sub_keys': nrm(ks[11], (DEPTH, PEER_HEADS, 2, PEER_N_KEYS, PEER_HALF), PEER_HALF ** -0.5),
        'peer_u': nrm(ks[12], (DEPTH, PEER_N_EXPERTS, D_MODEL), D_MODEL ** -0.5),
        'peer_v': nrm(ks[13], (DEPTH, PEER_N_EXPERTS, D_MODEL), D_MODEL ** -0.5),
        'final_norm': 1.0 + nrm(ks[14], (D_MODEL,), 0.01),
    }

def reference(x, mixer_norm, attn_w_in, attn_sinks, attn_w_out, hgrn_w_in, hgrn_lb_raw, hgrn_out_norm,
              hgrn_w_out, ffn_norm, peer_w_q, peer_sub_keys, peer_u, peer_v, final_norm):
    lb = jnp.cumsum(jax.nn.softmax(hgrn_lb_raw.astype(jnp.float32), axis=0), axis=0)
    lb = lb - lb[0]
    h = x
    for i in range(DEPTH):
        xn = rmsnorm(h, mixer_norm[i])
        j = i // N_MIXERS
        if i % N_MIXERS == 0:
            h = h + swa_attention(xn, attn_w_in[j], attn_sinks[j], attn_w_out[j])
        else:
            h = h + hgrn2(xn, hgrn_w_in[j], lb[j], hgrn_out_norm[j], hgrn_w_out[j])
        h = h + peer_ffn(rmsnorm(h, ffn_norm[i]), peer_w_q[i], peer_sub_keys[i], peer_u[i], peer_v[i])
    return rmsnorm(h, final_norm)


_drawn_inputs = setup_inputs


def setup_inputs(seed=0):
    import zlib

    import numpy as np

    out = dict(_drawn_inputs(seed))
    spreads = {}
    factors = {'mixer_norm': 6.552,
     'attn_sinks': 8.0,
     'hgrn_out_norm': 42.442,
     'ffn_norm': 25.16,
     'peer_sub_keys': 2.669,
     'peer_u': 2.932,
     'final_norm': 33.047}
    for name, (base, spread) in spreads.items():
        noise = np.random.default_rng([zlib.crc32(name.encode()), seed]).standard_normal(out[name].shape)
        drawn = base * np.exp(spread * noise) if base else spread * noise
        out[name] = __import__('jax').numpy.asarray(drawn.astype(out[name].dtype))
    for name, factor in factors.items():
        out[name] = (out[name] * factor).astype(out[name].dtype)
    return out
```

```python
from contextlib import ExitStack

import numpy as np

import concourse.bass as bass
from concourse import mybir

F32 = mybir.dt.float32
U32 = mybir.dt.uint32
ALU = mybir.AluOpType
ACT = mybir.ActivationFunctionType
AX = mybir.AxisListType.X

P = 128
TILES = 2
D = 1024
KT = D // P
EPS = 1e-6
HALF = 512
ITERS = 4
STEPS = 8
GQ, HD = 4, 64
QK = (GQ + 1) * HD
AW = (GQ + 2) * HD
CHUNK = 64
BLOCKED = -3e38
HH = 2
LEVELS = 7
PH, KEYS, TOPK = 8, 128, 16
EXPERTS = KEYS * KEYS
RH = 2
RHC = RH * 2
SLOTS = 8
SUB = 2
SUBS_AHEAD = SLOTS // SUB
LOWEST = -3.4e38


class InOrder:

    def __init__(self, engine, done):
        self.engine, self.done, self.n = engine, done, 0

    def restart(self):
        self.engine.sem_clear(self.done)
        self.n = 0

    def __call__(self, instruction):
        self.n += 1
        instruction.then_inc(self.done, 1)
        self.engine.wait_ge(self.done, self.n)


def level_count(tile, i, level):
    per = LEVELS + 1
    return (i * per if tile == 0 else ITERS * per + i * (per + 1)) + level + 1


def trunk(nc, x, cos, sin, masks_attn, masks_hgrn, ident_in, iota_in, gains, sinks, lb_raw, out_gain,
          attn_in, attn_out, hgrn_in, hgrn_out, route_w, experts, out):
    with ExitStack() as ctx:
        def sb(name, shape, dtype=F32):
            return ctx.enter_context(nc.sbuf_tensor(name, shape, dtype))

        def ps(name, shape):
            return ctx.enter_context(nc.psum_tensor(name, shape, F32))

        def sem(name):
            return ctx.enter_context(nc.semaphore(name))

        ring = sb("ring", [P, SLOTS, 2 * D])
        wmix = sb("wmix", [P, 2, 5 * D])
        wroute = sb("wroute", [P, (KT + 1) * RHC * P])
        h = sb("h", [P, TILES, D])
        xn = sb("xn", [P, TILES, D])
        xT = sb("xT", [P, KT, P])
        gain = sb("gain", [P, 2, D])
        ident = sb("ident", [P, P])
        cos_t = sb("cos_t", [P, TILES, HD])
        sin_t = sb("sin_t", [P, TILES, HD])
        amask = sb("amask", [P, 128 + 192])
        hmask = sb("hmask", [P, LEVELS + 1, P], U32)
        iota16 = sb("iota16", [P, TOPK])
        sink_t = sb("sink_t", [P, 4 * GQ])
        lbr = sb("lbr", [P, 8])
        lbe = sb("lbe", [P, 8])
        lbp = sb("lbp", [P, 8])
        lb = sb("lb", [P, 8])
        one_lb = sb("one_lb", [P, 8])
        ogain = sb("ogain", [P, P])
        ss = sb("ss", [P, 1])
        ms = sb("ms", [P, 1])
        ims = sb("ims", [P, 1])
        rstd = sb("rstd", [P, 1])
        idx = sb("idx", [P, TILES, PH * TOPK], U32)
        idc = sb("idc", [P, TOPK], U32)
        gate = sb("gate", [P, TILES, PH * TOPK])
        gate_now = sb("gate_now", [P, TOPK])
        dots = sb("dots", [P, TOPK])
        gel = sb("gel", [P, TOPK])
        coef = sb("coef", [P, TOPK])
        diag = sb("diag", [P, SLOTS, P])
        mix = sb("mix", [P, 8064])
        at = [0]

        def part(words):
            at[0] += words
            assert at[0] <= 8064
            return mix[:, at[0] - words:at[0]]

        rot_c = part(QK)
        rot_s = part(QK)
        rqk = part(QK + HD)
        qkT = part(3 * P)
        qkv = part(AW)
        v_cur = qkv[:, QK:AW]
        v_prev = part(HD)
        k_prev = part(P)
        kA = part(ITERS * P)
        vA = part(ITERS * HD)
        sm = part(GQ * 192)
        prob = part(GQ * 2 * P)
        pT = part(GQ * 2 * P)
        a_on = part(GQ * HD)
        a_oT = part(GQ * HD)
        sink4 = part(GQ)
        mx = part(GQ)
        mxs = part(GQ)
        nm = part(GQ)
        sink_d = part(GQ)
        sink_e = part(GQ)
        den = part(GQ)
        den_s = part(GQ)
        rden = part(GQ)
        at[0] = 0
        sg = part(2 * HALF)
        hq = part(2 * P)
        hk = part(2 * P)
        pre = part(2 * P)
        suf = part(2 * P)
        qb = part(2 * 2 * P)
        kb = part(2 * 2 * P)
        hv = part(2 * P)
        gg = part(2 * P)
        gs = part(2 * P)
        scT = part(2 * P)
        scX = part(2 * P)
        h_on = part(2 * P)
        h_on2 = part(2 * P)
        h_oT = part(2 * P)
        KA = part(8 * P)
        VA = part(8 * P)
        KAc = part(2 * P)
        VAc = part(2 * P)
        lb2 = part(2)
        one_lb2 = part(2)
        hss = part(2)
        hms = part(2)
        him = part(2)
        hrs = part(2)
        rqT = sb("rqT", [P, RHC * P])
        sv = sb("sv", [P, RHC, TOPK])
        si = sb("si", [P, RHC, TOPK], U32)
        sif = sb("sif", [P, RHC, TOPK])
        rest = sb("rest", [P, RHC, KEYS])
        cand = sb("cand", [P, RH, TOPK * TOPK])
        crest = sb("crest", [P, RH, TOPK * TOPK])
        ci = sb("ci", [P, RH, TOPK], U32)
        cab = sb("cab", [P, 2, RH, TOPK], U32)
        cabf = sb("cabf", [P, 2, RH, TOPK])
        chosen = sb("chosen", [P, 2, RH, TOPK])
        expert = sb("expert", [P, RH, TOPK])
        cvt = sb("cvt", [P, RH, TOPK])
        cv = sb("cv", [P, PH * TOPK])
        cvs = sb("cvs", [P, PH * TOPK])
        ge = sb("ge", [P, PH * TOPK])
        gsum = sb("gsum", [P, PH])
        ginv = sb("ginv", [P, PH])

        acc = ps("acc", [P, D])
        y = ps("y", [P, D])
        pj = ps("pj", [P, 2, HALF])
        sc = ps("sc", [P, HALF])
        ob = ps("ob", [P, HALF])

        const_in = sem("const_in")
        gain_in = [sem("gain_in0"), sem("gain_in1")]
        wattn_in, wattn_out_in = sem("wattn_in"), sem("wattn_out_in")
        whgrn_in = [sem("whgrn_in0"), sem("whgrn_in1")]
        whgrn_out_in = sem("whgrn_out_in")
        wroute_in = sem("wroute_in")
        slot_in = [sem(f"slot_in{k}") for k in range(SLOTS)]
        out_done = sem("out_done")
        dve_done = sem("dve_done")
        passed = {n: sem(f"{n}_passed") for n in ("dve", "pool")}
        h_ready = sem("h_ready")
        ims_ready, rstd_ready, norm_done = sem("ims_ready"), sem("rstd_ready"), sem("norm_done")
        xT_ps, xT_act, xT_dve = sem("xT_ps"), sem("xT_act"), sem("xT_dve")
        lb_zero, lb_exp = sem("lb_zero"), sem("lb_exp")
        cleared = sem("cleared")
        idc_ready, dots_ready, gelu_ready = sem("idc_ready"), sem("dots_ready"), sem("gelu_ready")
        coef_ready, diag_ready, subs_free = sem("coef_ready"), sem("diag_ready"), sem("subs_free")
        a_proj, a_qkv, a_rope, a_qkT_ps, a_qkT = sem("a_proj"), sem("a_qkv"), sem("a_rope"), sem("a_qkT_ps"), sem("a_qkT")
        a_score, a_nm, a_prob, a_sink = sem("a_score"), sem("a_nm"), sem("a_prob"), sem("a_sink")
        a_pT_ps, a_pT_act, a_pT_dve = sem("a_pT_ps"), sem("a_pT_act"), sem("a_pT_dve")
        a_o, a_on_ready, a_oT_ps, a_oT_ready = sem("a_o"), sem("a_on_ready"), sem("a_oT_ps"), sem("a_oT_ready")
        a_outproj = sem("a_outproj")
        h_proj, h_act, h_factors, h_score = sem("h_proj"), sem("h_act"), sem("h_factors"), sem("h_score")
        h_scT, h_o, h_sq, h_ims, h_rstd = sem("h_scT"), sem("h_o"), sem("h_sq"), sem("h_ims"), sem("h_rstd")
        h_on_ready, h_oT_ps, h_oT_ready = sem("h_on_ready"), sem("h_oT_ps"), sem("h_oT_ready")
        h_outproj = sem("h_outproj")
        r_proj, r_qT, r_score, r_done = sem("r_proj"), sem("r_qT"), sem("r_score"), sem("r_done")
        g_shift, g_exp, g_done = sem("g_shift"), sem("g_exp"), sem("g_done")

        CONSTS = ((ident[:], ident_in), (cos_t[:], cos), (sin_t[:], sin), (amask[:], masks_attn),
                  (hmask[:], masks_hgrn), (iota16[:], iota_in.to_broadcast([P, TOPK])),
                  (sink_t[:], sinks.to_broadcast([P, 4 * GQ])), (lbr[:], lb_raw),
                  (ogain[:], out_gain.to_broadcast([P, P])), (h[:, 0], x[0]), (h[:, 1], x[1]))
        CONST_BYTES_IN = 16 * len(CONSTS)

        PHASES = [(-1, None, (0, 0)), (0, (0, 0), (0, 1)), (1, (0, 1), (1, 0)), (2, (1, 0), (1, 1)),
                  (3, (1, 1), None)]

        def hold(engine, name, semaphore, value):
            engine.wait_ge(semaphore, value)
            engine.sem_inc(passed[name], 1)

        def h_count(phase):
            return 0 if phase < 0 else 2 * phase + 1

        def bands(ap, n):
            return ap.rearrange("p (n w) -> p n w", n=n)

        def window(tile):
            return (128, amask[:, 0:128]) if tile == 0 else (192, amask[:, 128:320])

        block = ctx.enter_context(nc.Block())

        @block.sync
        def _(sp):
            def load_mixer(layer, tile, i, first):
                n = tile * ITERS + i
                if layer == 0:
                    if not first:
                        sp.wait_ge(a_proj, n)
                    sp.dma_start(wmix[:, 0, 0:KT * AW], attn_in[bass.ds(i, 1)].squeeze(0)).then_inc(wattn_in, 16)
                    if not first:
                        sp.wait_ge(a_outproj, n)
                    sp.dma_start(wmix[:, 1, 0:2 * D], attn_out[bass.ds(i, 1)].squeeze(0)).then_inc(wattn_out_in, 16)
                    return
                for j in range(HH):
                    if first:
                        sp.wait_ge(a_proj, TILES * ITERS)
                        sp.wait_ge(a_outproj, TILES * ITERS)
                    else:
                        sp.wait_ge(h_proj, n * 2 - 1 + j)
                    sp.dma_start(wmix[:, j, 0:KT * HALF], hgrn_in[bass.ds(i * 2 + j, 1)].squeeze(0)).then_inc(whgrn_in[j], 16)
                if not first:
                    sp.wait_ge(h_outproj, n)
                sp.dma_start(wmix[:, :, KT * HALF:5 * D], hgrn_out[bass.ds(i, 1)].squeeze(0)).then_inc(whgrn_out_in, 16)

            def load_route(layer, tile, i, first=False):
                n = (layer * TILES + tile) * ITERS + i
                if not first:
                    sp.wait_ge(r_score, n)
                sp.dma_start(wroute[:], route_w[bass.ds(layer * ITERS + i, 1)].squeeze(0)).then_inc(wroute_in, 16)

            def load_gain(n):
                if n >= 2:
                    sp.wait_ge(norm_done, n - 1)
                row = (0, 2, 0, 2, 1, 3, 1, 3, 4, 4)[n]
                sp.dma_start(gain[:, n % 2], gains[row:row + 1].to_broadcast([P, D])).then_inc(gain_in[n % 2], 16)

            for to, of in reversed(CONSTS):
                sp.dma_start(to, of).then_inc(const_in, 16)
            load_gain(0)
            load_mixer(0, 0, 0, True)
            load_gain(1)
            for phase, _g, work in PHASES:
                if work is None:
                    continue
                layer, tile = work
                load_route(layer, tile, 0, first=phase < 0)
                with sp.Fori(1, ITERS) as i:
                    load_mixer(layer, tile, i, False)
                mix_norm = 2 * (phase + 1)
                load_gain(mix_norm + 2)
                if phase < 2:
                    load_mixer(*PHASES[phase + 2][2], 0, phase == 0)
                load_gain(mix_norm + 3)
                with sp.Fori(1, ITERS) as i:
                    load_route(layer, tile, i)
            for tile in range(TILES):
                sp.wait_ge(norm_done, 9 + tile)
                sp.dma_start(out[tile], xn[:, tile]).then_inc(out_done, 16)
            sp.wait_ge(out_done, 16 * TILES)

        @block.gpsimd
        def _(pool):
            for phase, gathered, _w in PHASES:
                if gathered is None:
                    continue
                layer, tile = gathered
                pool.wait_ge(r_done, (phase + 1) * ITERS)
                with pool.Fori(0, PH) as i:
                    for part_ in range(2):
                        cols = slice(part_ * SLOTS, (part_ + 1) * SLOTS)
                        pool.tensor_copy(idc[:, cols], idx[:, tile, bass.ds(i * TOPK + part_ * SLOTS, SLOTS)]).then_inc(idc_ready, 1)
                        hold(pool, "pool", idc_ready, (phase * PH + i) * 2 + part_ + 1)
                        for s in range(SUBS_AHEAD):
                            hold(pool, "pool", subs_free, (phase * PH + i) * STEPS + part_ * SUBS_AHEAD + s + 1)
                            for k in range(s * SUB, (s + 1) * SUB):
                                col = part_ * SLOTS + k
                                pool.indirect_dma_start(
                                    out=ring[:, k, :], out_offset=None, in_=experts,
                                    in_offset=bass.IndirectOffsetOnAxis(ap=idc[:, col:col + 1], axis=0),
                                ).then_inc(slot_in[k], 16)

        @block.scalar
        def _(act):
            def copy(to, of):
                return act.activation(to, of, ACT.Copy)

            def norm(n, transposed):
                act.wait_ge(ims_ready, n + 1)
                act.activation(rstd[:], ims[:], ACT.Sqrt).then_inc(rstd_ready, 1)
                if transposed:
                    act.wait_ge(xT_ps, n + 1)
                    copy(xT[:, 0:4], pj[:, 0].rearrange("p (k t) -> p k t", k=4)).then_inc(xT_act, 1)

            def attention(tile, i, s):
                n = tile * ITERS + i
                if s == 0:
                    act.wait_ge(a_proj, n + 1)
                    if tile == 0:
                        copy(vA[:, bass.ds(i * HD, HD)], pj[:, 0, QK:AW])
                    else:
                        copy(v_prev, vA[:, bass.ds(i * HD, HD)])
                        copy(k_prev, kA[:, bass.ds(i * P, P)])
                    copy(qkv, pj[:, 0, 0:AW]).then_inc(a_qkv, 1)
                elif s == 1:
                    act.wait_ge(a_qkT_ps, n + 1)
                    if tile == 0:
                        copy(kA[:, bass.ds(i * P, P)], ob[:, 2 * P:3 * P])
                    copy(qkT, ob[:, 0:3 * P]).then_inc(a_qkT, 1)
                elif s == 2:
                    act.wait_ge(a_nm, n + 1)
                    w, _ = window(tile)
                    for g in range(GQ):
                        act.activation(bands(prob, GQ)[:, g, 2 * P - w:2 * P], bands(sm, GQ)[:, g, 0:w], ACT.Exp,
                                       bias=nm[:, g:g + 1], accum_out=den[:, g:g + 1]).then_inc(a_prob, 1)
                    act.activation(sink_e, sink_d, ACT.Exp).then_inc(a_sink, 1)
                elif s == 3:
                    act.wait_ge(a_pT_ps, n + 1)
                    copy(pT[:, 0:HALF], pj[:, 0]).then_inc(a_pT_act, 1)
                elif s == 5:
                    act.wait_ge(a_oT_ps, n + 1)
                    copy(a_oT, sc[:, 256:512]).then_inc(a_oT_ready, 1)

            def hgrn(tile, i, s):
                n = tile * ITERS + i
                if s == 1:
                    act.wait_ge(h_proj, 2 * n + 2)
                    copy(bands(hv, 2), pj[:, :, 256:384])
                    if tile == 0:
                        copy(bands(VA[:, bass.ds(i * 2 * P, 2 * P)], 2), pj[:, :, 256:384])
                    else:
                        copy(KAc, KA[:, bass.ds(i * 2 * P, 2 * P)])
                        copy(VAc, VA[:, bass.ds(i * 2 * P, 2 * P)])
                    act.activation(bands(sg, 2), pj[:, :, :], ACT.Sigmoid).then_inc(h_act, 1)
                elif s == 6:
                    act.wait_ge(h_o, n + 1)
                    for j in range(HH):
                        act.activation(h_on[:, j * P:(j + 1) * P], ob[:, j * P:(j + 1) * P], ACT.Square,
                                       accum_out=hss[:, j:j + 1]).then_inc(h_sq, 1)
                    act.wait_ge(h_ims, n + 1)
                    act.activation(hrs, him, ACT.Sqrt).then_inc(h_rstd, 1)
                elif s == 7:
                    act.wait_ge(h_oT_ps, n + 1)
                    copy(h_oT, ob[:, 256:512]).then_inc(h_oT_ready, 1)

            def routing(n, s):
                if s == 1:
                    act.wait_ge(r_proj, n + 1)
                    copy(rqT[:], pj[:, 0]).then_inc(r_qT, 1)

            def step(g, s, beside):
                if g is not None:
                    act.wait_ge(dots_ready, g * STEPS + s + 1)
                    act.activation(gel[:, s * SUB:(s + 1) * SUB], dots[:, s * SUB:(s + 1) * SUB], ACT.Gelu).then_inc(gelu_ready, 1)
                beside()
                if g is not None:
                    act.wait_ge(coef_ready, g * STEPS + s + 1)
                    for k in range(s * SUB, (s + 1) * SUB):
                        last = act.activation(diag[:, k % SLOTS], ident[:], ACT.Copy, scale=coef[:, k:k + 1])
                    last.then_inc(diag_ready, 1)

            act.wait_ge(lb_zero, 1)
            act.activation(lbe[:], lbp[:], ACT.Exp).then_inc(lb_exp, 1)
            for phase, gathered, work in PHASES:
                mix_norm = 2 * (phase + 1)
                norm(mix_norm, work is not None)
                with act.Fori(0, ITERS) as i:
                    for s in range(STEPS):
                        g = phase * PH + i if gathered else None
                        if work is None:
                            step(g, s, lambda: None)
                        elif work[0] == 0:
                            step(g, s, lambda: attention(work[1], i, s))
                        else:
                            step(g, s, lambda: hgrn(work[1], i, s))
                if work is not None:
                    norm(mix_norm + 1, True)
                with act.Fori(0, ITERS) as i:
                    for s in range(STEPS):
                        g = phase * PH + ITERS + i if gathered else None
                        step(g, s, (lambda: None) if work is None else (lambda: routing((phase + 1) * ITERS + i, s)))
                if work is not None:
                    act.wait_ge(g_shift, phase + 2)
                    act.activation(ge[:], cvs[:], ACT.Exp).then_inc(g_exp, 1)
            norm(9, False)

        @block.vector
        def _(dve):
            link = InOrder(dve, dve_done)

            def norm(n, tile, transposed):
                dve.wait_ge(gain_in[n % 2], 16 * (n // 2 + 1))
                link(dve.tensor_tensor_reduce(out=xn[:, tile], in0=h[:, tile], in1=h[:, tile], scale=1.0, scalar=0.0,
                                              op0=ALU.mult, op1=ALU.add, accum_out=ss[:]))
                link(dve.tensor_scalar(ms[:], ss[:], 1.0 / D, EPS, ALU.mult, ALU.add))
                dve.reciprocal(ims[:], ms[:]).then_inc(ims_ready, 1)
                dve.wait_ge(rstd_ready, n + 1)
                dve.scalar_tensor_tensor(xn[:, tile], h[:, tile], rstd[:], gain[:, n % 2], ALU.mult, ALU.mult).then_inc(norm_done, 1)
                if transposed:
                    dve.wait_ge(xT_ps, n + 1)
                    dve.tensor_copy(xT[:, 4:8], pj[:, 1].rearrange("p (k t) -> p k t", k=4)).then_inc(xT_dve, 1)

            def attention(tile, i, s):
                n = tile * ITERS + i
                w, mask = window(tile)
                if s == 0:
                    hold(dve, "dve", a_qkv, n + 1)
                    dve.tensor_copy(sink4, sink_t[:, bass.ds(i * GQ, GQ)])
                    qk = bands(qkv[:, 0:QK], GQ + 1)
                    heads = [P, GQ + 1, HD // 2]
                    c, sn = cos_t[:, tile].unsqueeze(1), sin_t[:, tile].unsqueeze(1)
                    dve.tensor_tensor(bands(rot_c, GQ + 1), qk, c.broadcast_to([P, GQ + 1, HD]), ALU.mult)
                    dve.tensor_tensor(bands(rot_s, GQ + 1)[:, :, 0:32], qk[:, :, 32:64], sn[:, :, 0:32].broadcast_to(heads), ALU.mult)
                    link(dve.tensor_tensor(bands(rot_s, GQ + 1)[:, :, 32:64], qk[:, :, 0:32], sn[:, :, 32:64].broadcast_to(heads), ALU.mult))
                    dve.tensor_tensor(rqk[:, 0:QK], rot_c, rot_s, ALU.add)
                    dve.tensor_tensor(rqk[:, QK:QK + HD], rot_c[:, QK - HD:QK], rot_s[:, QK - HD:QK], ALU.add).then_inc(a_rope, 1)
                elif s == 2:
                    hold(dve, "dve", a_score, n + 1)
                    for half, bank in ((0, pj[:, 1]), (1, sc)):
                        last = dve.scalar_tensor_tensor(
                            bands(sm, GQ)[:, half:GQ:2, 0:w], bank[:, 0:2 * w].rearrange("p (n w) -> p n w", n=2),
                            HD ** -0.5, mask.unsqueeze(1).broadcast_to([P, 2, w]), ALU.mult, ALU.add)
                    link(last)
                    link(dve.reduce_max(mx, bands(sm, GQ)[:, :, 0:w], AX))
                    link(dve.tensor_tensor(mxs, mx, sink4, ALU.max))
                    dve.tensor_tensor(sink_d, sink4, mxs, ALU.subtract)
                    dve.tensor_scalar(nm, mxs, -1.0, None, ALU.mult).then_inc(a_nm, 1)
                elif s == 3:
                    hold(dve, "dve", a_sink, n + 1)
                    link(dve.tensor_tensor(den_s, den, sink_e, ALU.add))
                    link(dve.reciprocal(rden, den_s))
                    hold(dve, "dve", a_pT_ps, n + 1)
                    dve.tensor_copy(pT[:, HALF:D], ob[:]).then_inc(a_pT_dve, 1)
                elif s == 4:
                    hold(dve, "dve", a_o, n + 1)
                    dve.tensor_tensor(bands(a_on, GQ), bands(sc[:, 0:GQ * HD], GQ), rden.unsqueeze(2).broadcast_to([P, GQ, HD]),
                                      ALU.mult).then_inc(a_on_ready, 1)

            def hgrn(tile, i, s):
                n = tile * ITERS + i

                def produce(level):
                    if level == 0:
                        return
                    side = level % 2
                    if level <= LEVELS:
                        dve.tensor_tensor(bands(kb, 2)[:, side], hk, suf, ALU.mult)
                    dve.tensor_tensor(bands(qb, 2)[:, side], hq, pre, ALU.mult).then_inc(h_factors, 1)
                    if level > LEVELS:
                        return
                    hold(dve, "dve", h_factors, level_count(tile, i, level))
                    b = 1 << (level - 1)
                    blocks = 2 * P // (2 * b)
                    pv = pre.rearrange("p (n two b) -> p n two b", two=2, b=b)
                    sv_ = suf.rearrange("p (n two b) -> p n two b", two=2, b=b)
                    link(dve.tensor_tensor(sv_[:, :, 0], sv_[:, :, 0], pv[:, :, 1, b - 1:b].broadcast_to([P, blocks, b]), ALU.mult))
                    link(dve.tensor_tensor(pv[:, :, 1], pv[:, :, 1], pv[:, :, 0, b - 1:b].broadcast_to([P, blocks, b]), ALU.mult))

                def consume(level):
                    hold(dve, "dve", h_score, level_count(tile, i, level))
                    side = (sc, ob)[level % 2][:, 0:2 * P]
                    if level > LEVELS:
                        return dve.tensor_copy(scX, side)
                    return dve.copy_predicated(bands(scT, 2), hmask[:, level].unsqueeze(1).broadcast_to([P, 2, P]), bands(side, 2))

                if s == 2:
                    hold(dve, "dve", h_act, n + 1)
                    dve.tensor_copy(lb2, lb[:, bass.ds(i * 2, 2)])
                    link(dve.tensor_copy(one_lb2, one_lb[:, bass.ds(i * 2, 2)]))
                    for j in range(HH):
                        last = dve.tensor_scalar(pre[:, j * P:(j + 1) * P], sg[:, j * HALF + P:j * HALF + 2 * P], one_lb2[:, j:j + 1],
                                                 lb2[:, j:j + 1], ALU.mult, ALU.add)
                    link(last)
                    dve.tensor_scalar(hk, pre, -1.0, 1.0, ALU.mult, ALU.add)
                    dve.tensor_tensor(bands(hq, 2), pj[:, :, 0:P], bands(sg, 2)[:, :, 0:P], ALU.mult).then_inc(h_factors, 1)
                    hold(dve, "dve", h_factors, level_count(tile, i, 0))
                    link(dve.memset(suf, 1.0))
                    produce(1)
                    link(dve.tensor_tensor(bands(gs, 2), pj[:, :, 384:512], bands(sg, 2)[:, :, 384:512], ALU.mult))
                    dve.tensor_tensor(bands(gg, 2), bands(gs, 2), ogain[:].unsqueeze(1).broadcast_to([P, 2, P]), ALU.mult)
                    link(consume(0))
                elif s in (3, 4, 5):
                    for level in (2 * s - 4, 2 * s - 3):
                        produce(level)
                        link(consume(level - 1))
                elif s == 6:
                    if tile == 1:
                        produce(8)
                        link(consume(7))
                        consume(8).then_inc(h_scT, 1)
                    else:
                        link(dve.tensor_tensor(KA[:, bass.ds(i * 2 * P, 2 * P)], hk, suf, ALU.mult))
                        consume(7).then_inc(h_scT, 1)
                    hold(dve, "dve", h_sq, 2 * n + 2)
                    link(dve.tensor_scalar(hms, hss, 1.0 / P, EPS, ALU.mult, ALU.add))
                    dve.reciprocal(him, hms).then_inc(h_ims, 1)
                elif s == 7:
                    hold(dve, "dve", h_rstd, n + 1)
                    link(dve.tensor_tensor(bands(h_on2, 2), bands(ob[:, 0:256], 2), hrs.unsqueeze(2).broadcast_to([P, 2, P]), ALU.mult))
                    dve.tensor_tensor(h_on, h_on2, gg, ALU.mult).then_inc(h_on_ready, 1)

            def top16(values, indices, source, remaining, rows):
                for r in rows:
                    last = dve.max(values[:, r, 0:8], source[r])
                link(last)
                for r in rows:
                    dve.max_index(indices[:, r, 0:8], values[:, r, 0:8], source[r])
                    last = dve.match_replace(remaining[:, r], values[:, r, 0:8], source[r], LOWEST)
                link(last)
                for r in rows:
                    last = dve.max(values[:, r, 8:16], remaining[:, r])
                link(last)
                for r in rows:
                    last = dve.max_index(indices[:, r, 8:16], values[:, r, 8:16], remaining[:, r])
                link(last)

            def routing(layer, n, i, s):
                scores = [sc[:, c * KEYS:(c + 1) * KEYS] for c in range(RHC)]
                if s == 2:
                    hold(dve, "dve", r_score, n + 1)
                    top16(sv, si, scores, rest, (0, 1))
                elif s == 3:
                    top16(sv, si, scores, rest, (2, 3))
                elif s == 4:
                    dve.tensor_copy(sif[:], si[:])
                    by_half = sv[:].rearrange("p (h c) k -> p h c k", c=2)
                    grid = [P, RH, TOPK, TOPK]
                    link(dve.tensor_tensor(cand[:].rearrange("p h (a b) -> p h a b", b=TOPK),
                                           by_half[:, :, 0].unsqueeze(3).broadcast_to(grid),
                                           by_half[:, :, 1].unsqueeze(2).broadcast_to(grid), ALU.add))
                elif s == 5:
                    top16(cvt, ci, [cand[:, r] for r in range(RH)], crest, range(RH))
                elif s == 6:
                    dve.tensor_scalar(cab[:, 0], ci[:], 4, None, ALU.logical_shift_right)
                    link(dve.tensor_scalar(cab[:, 1], ci[:], TOPK - 1, None, ALU.bitwise_and))
                    link(dve.tensor_copy(cabf[:], cab[:]))
                    grid = [P, RH, TOPK, TOPK]
                    picks = [a[:].rearrange("p h (k a) -> p h k a", a=TOPK) for a in (cand, crest)]
                    for c in range(2):
                        last = dve.tensor_tensor(picks[c], cabf[:, c].unsqueeze(3).broadcast_to(grid),
                                                 iota16[:].unsqueeze(1).unsqueeze(1).broadcast_to(grid), ALU.is_equal)
                    link(last)
                    for c in range(2):
                        of_half = sif[:].rearrange("p (h c) k -> p h c k", c=2)[:, :, c]
                        last = dve.tensor_tensor(picks[c], picks[c], of_half.unsqueeze(2).broadcast_to(grid), ALU.mult)
                    link(last)
                    for c in range(2):
                        last = dve.reduce_sum(chosen[:, c], picks[c], AX)
                    link(last)
                    link(dve.scalar_tensor_tensor(expert[:], chosen[:, 0], float(KEYS), chosen[:, 1], ALU.mult, ALU.add))
                    here = bass.ds(i * RH * TOPK, RH * TOPK)
                    dve.tensor_copy(cv[:, here], cvt[:].rearrange("p h k -> p (h k)"))
                    tile = n_tile(n)
                    dve.tensor_scalar(idx[:, tile, here], expert[:].rearrange("p h k -> p (h k)"), float(layer * EXPERTS), None,
                                      ALU.add).then_inc(r_done, 1)
                    hold(dve, "dve", r_done, n + 1)

            tile_now = [0]

            def n_tile(_n):
                return tile_now[0]

            def gates(phase, tile):
                of_head = cv[:].rearrange("p (h k) -> p h k", k=TOPK)
                shape = [P, PH, TOPK]
                dve.tensor_tensor(cvs[:].rearrange("p (h k) -> p h k", k=TOPK), of_head, of_head[:, :, 0:1].broadcast_to(shape), ALU.subtract).then_inc(g_shift, 1)
                dve.wait_ge(g_exp, phase + 2)
                link(dve.reduce_sum(gsum[:], ge[:].rearrange("p (h k) -> p h k", k=TOPK), AX))
                link(dve.reciprocal(ginv[:], gsum[:]))
                dve.tensor_tensor(gate[:, tile].rearrange("p (h k) -> p h k", k=TOPK), ge[:].rearrange("p (h k) -> p h k", k=TOPK),
                                  ginv[:].unsqueeze(2).broadcast_to(shape), ALU.mult).then_inc(g_done, 1)
                dve.wait_ge(g_done, phase + 2)

            def gather_head(g, tile, i):
                link(dve.tensor_copy(gate_now[:], gate[:, tile, bass.ds(i * TOPK, TOPK)]))

            def step(g, round_, tile, s, beside):
                if g is not None:
                    for k in range(s * SUB, (s + 1) * SUB):
                        slot = k % SLOTS
                        hold(dve, "dve", slot_in[slot], (g * 2 + k // SLOTS + 1) * 16)
                        last = dve.tensor_tensor_reduce(out=ring[:, slot, 0:D], in0=ring[:, slot, 0:D], in1=xn[:, tile], scale=1.0,
                                                        scalar=0.0, op0=ALU.mult, op1=ALU.add, accum_out=dots[:, k:k + 1])
                    last.then_inc(dots_ready, 1)
                beside()
                if g is not None:
                    cols = slice(s * SUB, (s + 1) * SUB)
                    hold(dve, "dve", gelu_ready, g * STEPS + s + 1)
                    dve.tensor_tensor(coef[:, cols], gel[:, cols], gate_now[:, cols], ALU.mult).then_inc(coef_ready, 1)
                    if s == STEPS - 1:
                        hold(dve, "dve", coef_ready, (g + 1) * STEPS)

            dve.wait_ge(const_in, CONST_BYTES_IN)
            dve.tensor_tensor(lbp[:], lbr[:], lbr[:], ALU.subtract).then_inc(lb_zero, 1)
            dve.wait_ge(lb_exp, 1)
            link(dve.reciprocal(lbp[:], lbe[:]))
            link(dve.tensor_tensor(lbe[:], lbe[:], lbp[:], ALU.mult))
            link(dve.tensor_tensor(lb[:], lbe[:], lbe[:], ALU.subtract))
            link(dve.tensor_scalar(one_lb[:], lb[:], -1.0, 1.0, ALU.mult, ALU.add))
            dve.memset(prob, 0.0).then_inc(cleared, 1)
            for phase, gathered, work in PHASES:
                mix_norm = 2 * (phase + 1)
                if work is not None:
                    layer, tile = work
                    norm(mix_norm, tile, True)
                    if phase == 1:
                        link(dve.memset(scT, 0.0))
                else:
                    norm(mix_norm, 0, False)
                with dve.Fori(0, ITERS) as i:
                    link.restart()
                    g = phase * PH + i if gathered else None
                    if gathered:
                        gather_head(g, gathered[1], i)
                    for s in range(STEPS):
                        if work is None:
                            step(g, 0, gathered[1], s, lambda: None)
                        else:
                            step(g, 0, gathered and gathered[1], s,
                                 (lambda: attention(tile, i, s)) if layer == 0 else (lambda: hgrn(tile, i, s)))
                if work is not None:
                    dve.wait_ge(*((a_outproj, (tile + 1) * ITERS) if layer == 0 else (h_outproj, (tile + 1) * ITERS)))
                    dve.tensor_copy(h[:, tile], y[:]).then_inc(h_ready, 1)
                    dve.wait_ge(h_ready, h_count(phase) + 1)
                    norm(mix_norm + 1, tile, True)
                    tile_now[0] = tile
                with dve.Fori(0, ITERS) as i:
                    link.restart()
                    g = phase * PH + ITERS + i if gathered else None
                    if gathered:
                        gather_head(g, gathered[1], i + ITERS)
                    for s in range(STEPS):
                        if work is None:
                            step(g, 0, gathered[1], s, lambda: None)
                        else:
                            step(g, 0, gathered and gathered[1], s, lambda: routing(layer, (phase + 1) * ITERS + i, i, s))
                if work is not None:
                    gates(phase, tile)
                if gathered:
                    dve.wait_ge(subs_free, (phase + 1) * PH * STEPS + SUBS_AHEAD)
                    dve.tensor_copy(h[:, gathered[1]], acc[:]).then_inc(h_ready, 1)
                    dve.wait_ge(h_ready, h_count(phase) + (2 if work is not None else 1))
            norm(9, 1, False)

        @block.tensor
        def _(pe):
            def norm(n, tile):
                pe.wait_ge(norm_done, n + 1)
                for k in range(KT):
                    last = nc.tensor.transpose(pj[:, k // 4, k % 4 * P:k % 4 * P + P], xn[:, tile, k * P:(k + 1) * P], ident[:])
                last.then_inc(xT_ps, 1)
                pe.wait_ge(xT_act, n + 1)
                pe.wait_ge(xT_dve, n + 1)

            def residual(bank, tile):
                for j in range(2):
                    last = nc.tensor.matmul(bank[:, j * HALF:(j + 1) * HALF], ident[:], h[:, tile, j * HALF:(j + 1) * HALF], start=True, stop=True)
                return last

            def attention(tile, i, s):
                n = tile * ITERS + i
                w, _ = window(tile)
                if s == 0:
                    pe.wait_ge(wattn_in, 16 * (n + 1))
                    for k in range(KT):
                        last = nc.tensor.matmul(pj[:, 0, 0:AW], xT[:, k], wmix[:, 0, k * AW:(k + 1) * AW], start=k == 0, stop=k == KT - 1)
                    last.then_inc(a_proj, 1)
                elif s == 1:
                    pe.wait_ge(a_rope, n + 1)
                    for c in range(3):
                        last = nc.tensor.transpose(ob[:, c * P:(c + 1) * P], rqk[:, c * P:(c + 1) * P], ident[:])
                    last.then_inc(a_qkT_ps, 1)
                elif s == 2:
                    pe.wait_ge(a_qkT, n + 1)
                    for g in range(GQ):
                        bank = (pj[:, 1], sc)[g % 2]
                        rows = slice(g % 2 * HD, g % 2 * HD + HD)
                        q = qkT[rows, g // 2 * P:(g // 2 + 1) * P]
                        at_ = g // 2 * w
                        if tile == 1:
                            nc.tensor.matmul(bank[:, at_:at_ + CHUNK], q, k_prev[rows, CHUNK:P], start=True, stop=True)
                        last = nc.tensor.matmul(bank[:, at_ + w - P:at_ + w], q, qkT[rows, 2 * P:3 * P], start=True, stop=True)
                    last.then_inc(a_score, 1)
                elif s == 3:
                    pe.wait_ge(a_prob, GQ * (n + 1))
                    for g in range(GQ):
                        bank = pj[:, 0] if g < 2 else ob
                        for b in range(2):
                            to = (g % 2 * 2 + b) * P
                            last = nc.tensor.transpose(bank[:, to:to + P], prob[:, (g * 2 + b) * P:(g * 2 + b + 1) * P], ident[:])
                    last.then_inc(a_pT_ps, 1)
                elif s == 4:
                    pe.wait_ge(a_pT_act, n + 1)
                    pe.wait_ge(a_pT_dve, n + 1)
                    for g in range(GQ):
                        to = sc[:, g * HD:(g + 1) * HD]
                        if tile == 1:
                            nc.tensor.matmul(to, pT[:, g * 2 * P:(g * 2 + 1) * P], v_prev, start=True, stop=False)
                        last = nc.tensor.matmul(to, pT[:, (g * 2 + 1) * P:(g * 2 + 2) * P], v_cur, start=tile == 0, stop=True)
                    last.then_inc(a_o, 1)
                elif s == 5:
                    pe.wait_ge(a_on_ready, n + 1)
                    for c in range(2):
                        last = nc.tensor.transpose(sc[:, 256 + c * P:256 + (c + 1) * P], a_on[:, c * P:(c + 1) * P], ident[:])
                    last.then_inc(a_oT_ps, 1)
                elif s == 6:
                    pe.wait_ge(a_oT_ready, n + 1)
                    pe.wait_ge(wattn_out_in, 16 * (n + 1))
                    for c in range(2):
                        for j in range(2):
                            last = nc.tensor.matmul(y[:, j * HALF:(j + 1) * HALF], a_oT[:, c * P:(c + 1) * P],
                                                    wmix[:, 1, c * D + j * HALF:c * D + (j + 1) * HALF], start=False, stop=True,
                                                    skip_group_check=True)
                    last.then_inc(a_outproj, 1)

            def hgrn(tile, i, s):
                n = tile * ITERS + i

                def scores(level):
                    pe.wait_ge(h_factors, level_count(tile, i, level))
                    bank = (sc, ob)[level % 2]
                    side = level % 2 * 256
                    for j in range(HH):
                        cols = slice(side + j * P, side + (j + 1) * P)
                        own = slice(j * P, (j + 1) * P)
                        keys = hk[:, own] if level == 0 else KAc[:, own] if level > LEVELS else kb[:, cols]
                        last = nc.tensor.matmul(bank[:, own], keys, hq[:, own] if level == 0 else qb[:, cols], start=True, stop=True)
                    last.then_inc(h_score, 1)

                if s < 2:
                    pe.wait_ge(whgrn_in[s], 16 * (n + 1))
                    for c in range(2):
                        for k in range(KT):
                            nc.tensor.matmul(pj[:, s, c * P:(c + 1) * P], wmix[:, s, k * HALF + c * P:k * HALF + (c + 1) * P], xT[:, k],
                                             start=k == 0, stop=k == KT - 1)
                    for k in range(KT):
                        last = nc.tensor.matmul(pj[:, s, 256:512], xT[:, k], wmix[:, s, k * HALF + 256:(k + 1) * HALF],
                                                start=k == 0, stop=k == KT - 1)
                    last.then_inc(h_proj, 1)
                elif s < 6:
                    scores(2 * s - 4)
                    scores(2 * s - 3)
                elif s == 6:
                    if tile == 1:
                        scores(8)
                    pe.wait_ge(h_scT, n + 1)
                    for j in range(HH):
                        own = slice(j * P, (j + 1) * P)
                        last = nc.tensor.matmul(ob[:, own], scT[:, own], hv[:, own], start=True, stop=tile == 0)
                        if tile == 1:
                            last = nc.tensor.matmul(ob[:, own], scX[:, own], VAc[:, own], start=False, stop=True)
                    last.then_inc(h_o, 1)
                else:
                    pe.wait_ge(h_on_ready, n + 1)
                    for j in range(HH):
                        last = nc.tensor.transpose(ob[:, 256 + j * P:256 + (j + 1) * P], h_on[:, j * P:(j + 1) * P], ident[:])
                    last.then_inc(h_oT_ps, 1)
                    pe.wait_ge(h_oT_ready, n + 1)
                    pe.wait_ge(whgrn_out_in, 16 * (n + 1))
                    for c in range(HH):
                        for j in range(2):
                            last = nc.tensor.matmul(y[:, j * HALF:(j + 1) * HALF], h_oT[:, c * P:(c + 1) * P],
                                                    wmix[:, c, KT * HALF + j * HALF:KT * HALF + (j + 1) * HALF], start=False, stop=True,
                                                    skip_group_check=True)
                    last.then_inc(h_outproj, 1)

            def routing(n, s):
                if s < 2:
                    if s == 0:
                        pe.wait_ge(wroute_in, 16 * (n + 1))
                    for c in (2 * s, 2 * s + 1):
                        for k in range(KT):
                            last = nc.tensor.matmul(pj[:, 0, c * P:(c + 1) * P], wroute[:, (k * RHC + c) * P:(k * RHC + c + 1) * P], xT[:, k],
                                                    start=k == 0, stop=k == KT - 1)
                    if s == 1:
                        last.then_inc(r_proj, 1)
                elif s == 2:
                    pe.wait_ge(r_qT, n + 1)
                    for c in range(RHC):
                        last = nc.tensor.matmul(sc[:, c * KEYS:(c + 1) * KEYS], rqT[:, c * P:(c + 1) * P],
                                                wroute[:, (KT * RHC + c) * P:(KT * RHC + c + 1) * P], start=True, stop=True)
                    last.then_inc(r_score, 1)
                elif s == 7:
                    pe.wait_ge(r_done, n + 1)

            def step(g, s):
                pe.wait_ge(diag_ready, g * STEPS + s + 1)
                for k in range(s * SUB, (s + 1) * SUB):
                    slot = k % SLOTS
                    for j in range(2):
                        last = nc.tensor.matmul(acc[:, j * HALF:(j + 1) * HALF], diag[:, slot], ring[:, slot, D + j * HALF:D + (j + 1) * HALF],
                                                start=False, stop=True, skip_group_check=True)
                last.then_inc(subs_free, 1)

            pe.wait_ge(const_in, CONST_BYTES_IN)
            pe.wait_ge(cleared, 1)
            for phase, gathered, work in PHASES:
                mix_norm = 2 * (phase + 1)
                if phase >= 0:
                    pe.wait_ge(h_ready, h_count(phase))
                if gathered:
                    last = residual(acc, gathered[1])
                    if phase == 0:
                        last.then_inc(subs_free, SUBS_AHEAD)
                if work is not None:
                    residual(y, work[1])
                    norm(mix_norm, work[1])
                with pe.Fori(0, ITERS) as i:
                    for s in range(STEPS):
                        if work is not None:
                            (attention if work[0] == 0 else hgrn)(work[1], i, s)
                        if gathered:
                            step(phase * PH + i, s)
                if work is not None:
                    norm(mix_norm + 1, work[1])
                with pe.Fori(0, ITERS) as i:
                    for s in range(STEPS):
                        if work is not None:
                            routing((phase + 1) * ITERS + i, s)
                        if gathered:
                            step(phase * PH + ITERS + i, s)


def shape_constants():
    pos = np.arange(TILES * P, dtype=np.float32)[:, None]
    freq = np.float32(10000.0) ** (-np.arange(0, HD, 2, dtype=np.float32) / np.float32(HD))
    angle = (pos * freq[None]).astype(np.float32)
    c, s = np.cos(angle), np.sin(angle)
    cos = np.concatenate([c, c], 1).reshape(TILES, P, HD).transpose(1, 0, 2)
    sin = np.concatenate([-s, s], 1).reshape(TILES, P, HD).transpose(1, 0, 2)
    attn = np.zeros((P, 320), np.float32)
    attn[:CHUNK, CHUNK:128] = BLOCKED
    attn[:CHUNK, 128 + 128:] = BLOCKED
    attn[CHUNK:, 128:128 + CHUNK] = BLOCKED
    s_, t_ = np.arange(P)[:, None], np.arange(P)[None, :]
    hgrn = [s_ == t_]
    for level in range(LEVELS):
        b = 1 << level
        hgrn.append((s_ // (2 * b) == t_ // (2 * b)) & (s_ % (2 * b) < b) & (t_ % (2 * b) >= b))
    return {
        "cos": np.ascontiguousarray(cos, np.float32), "sin": np.ascontiguousarray(sin, np.float32),
        "masks_attn": attn, "masks_hgrn": np.ascontiguousarray(np.stack(hgrn, 1).astype(np.uint32)),
        "ident_in": np.eye(P, dtype=np.float32), "iota_in": np.arange(TOPK, dtype=np.float32)[None],
    }


def lay_out(a):
    def rows_by_partition(w):
        return w.reshape(-1, P, w.shape[-1]).transpose(1, 0, 2)

    w = a["attn_w_in"][0]
    q, k, v = w[:, :1024], w[:, 1024:1280], w[:, 1280:]
    attn_in = np.stack([rows_by_partition(np.concatenate(
        [q[:, g * 256:(g + 1) * 256], k[:, g * 64:(g + 1) * 64], v[:, g * 64:(g + 1) * 64]], 1)).reshape(P, -1) for g in range(4)])
    attn_out = a["attn_w_out"][0].reshape(4, 2, P, D).transpose(0, 2, 1, 3).reshape(4, P, 2 * D)
    w = a["hgrn_w_in"][0].reshape(KT, P, 4, 8, P)
    hgrn_in = w.transpose(3, 1, 0, 2, 4).reshape(8, P, KT * HALF)
    hgrn_out = a["hgrn_w_out"][0].reshape(4, HH, P, D).transpose(0, 2, 1, 3)
    wq = a["peer_w_q"].reshape(2, KT, P, ITERS, RHC, P).transpose(0, 3, 2, 1, 4, 5).reshape(2 * ITERS, P, -1)
    keys = a["peer_sub_keys"].reshape(2, ITERS, RHC, KEYS, P).transpose(0, 1, 4, 2, 3).reshape(2 * ITERS, P, -1)
    return {
        "x": a["x"].reshape(TILES, P, D),
        "gains": np.concatenate([a["mixer_norm"], a["ffn_norm"], a["final_norm"][None]]),
        "sinks": a["attn_sinks"], "lb_raw": a["hgrn_lb_raw"][0].reshape(8, P).T, "out_gain": a["hgrn_out_norm"],
        "attn_in": attn_in, "attn_out": attn_out, "hgrn_in": hgrn_in, "hgrn_out": hgrn_out,
        "route_w": np.concatenate([wq, keys], 2),
        "experts": np.concatenate([a["peer_u"], a["peer_v"]], 2).reshape(2 * EXPERTS, 2 * D),
    }


_ORDER = ["x", "cos", "sin", "masks_attn", "masks_hgrn", "ident_in", "iota_in", "gains", "sinks", "lb_raw", "out_gain",
          "attn_in", "attn_out", "hgrn_in", "hgrn_out", "route_w", "experts"]


def kernel(**inputs):
    import concourse.bacc as bacc
    from concourse.bass_utils import run_bass_kernel_spmd

    arrays = {**lay_out({n: np.asarray(v) for n, v in inputs.items()}), **shape_constants()}
    arrays = {n: np.ascontiguousarray(v) for n, v in arrays.items()}
    nc = bacc.Bacc("TRN2", target_bir_lowering=False, num_devices=1)
    args = [nc.dram_tensor(n, arrays[n].shape, mybir.dt.from_np(arrays[n].dtype), kind="ExternalInput").ap() for n in _ORDER]
    args.append(nc.dram_tensor("out", (TILES, P, D), F32, kind="ExternalOutput").ap())
    trunk(nc, *args)
    r = run_bass_kernel_spmd(nc, [arrays], core_ids=[0])
    return r.results[0]["out"].reshape(1, TILES * P, D)
```

```python
from contextlib import ExitStack

import numpy as np

import concourse.bass as bass
from concourse import mybir

F32 = mybir.dt.float32
U32 = mybir.dt.uint32
ALU = mybir.AluOpType
ACT = mybir.ActivationFunctionType
AX = mybir.AxisListType.X

P = 128
TILES = 2
D = 1024
KT = D // P
EPS = 1e-6
HALF = 512
ITERS = 4
STEPS = 8
GQ, HD = 4, 64
QK = (GQ + 1) * HD
AW = (GQ + 2) * HD
CHUNK = 64
BLOCKED = -3e38
HH = 2
LEVELS = 7
PH, KEYS, TOPK = 8, 128, 16
EXPERTS = KEYS * KEYS
RH = 2
RHC = RH * 2
SLOTS = 8
SUB = 2
LOWEST = -3.4e38


class InOrder:

    def __init__(self, engine, done):
        self.engine, self.done, self.n = engine, done, 0

    def restart(self):
        self.engine.sem_clear(self.done)
        self.n = 0

    def __call__(self, instruction):
        self.n += 1
        instruction.then_inc(self.done, 1)
        self.engine.wait_ge(self.done, self.n)


def level_count(tile, i, level):
    per = LEVELS + 1
    return (i * per if tile == 0 else ITERS * per + i * (per + 1)) + level + 1


def trunk(nc, x, cos, sin, masks_attn, masks_hgrn, ident_in, iota_in, gains, sinks, lb_raw, out_gain,
          attn_in, attn_out, hgrn_in, hgrn_out, route_w, experts, out):
    with ExitStack() as ctx:
        def sb(name, shape, dtype=F32):
            return ctx.enter_context(nc.sbuf_tensor(name, shape, dtype))

        def ps(name, shape):
            return ctx.enter_context(nc.psum_tensor(name, shape, F32))

        def sem(name):
            return ctx.enter_context(nc.semaphore(name))

        ring = sb("ring", [P, SLOTS, 2 * D])
        wmix = sb("wmix", [P, 2, 5 * D])
        wroute = sb("wroute", [P, (KT + 1) * RHC * P])
        h = sb("h", [P, TILES, D])
        xn = sb("xn", [P, TILES, D])
        xTs = sb("xTs", [P, 2, KT, P])
        xT, xT_route = xTs[:, 0], xTs[:, 1]
        gain = sb("gain", [P, 2, D])
        ident = sb("ident", [P, P])
        cos_t = sb("cos_t", [P, TILES, HD])
        sin_t = sb("sin_t", [P, TILES, HD])
        amask = sb("amask", [P, 128 + 192])
        hmask = sb("hmask", [P, LEVELS + 1, P], U32)
        iota16 = sb("iota16", [P, TOPK])
        sink_t = sb("sink_t", [P, 4 * GQ])
        lbr = sb("lbr", [P, 8])
        lbe = sb("lbe", [P, 8])
        lbp = sb("lbp", [P, 8])
        lb = sb("lb", [P, 8])
        one_lb = sb("one_lb", [P, 8])
        ogain = sb("ogain", [P, P])
        ss = sb("ss", [P, 1])
        ms = sb("ms", [P, 1])
        ims = sb("ims", [P, 1])
        rstd = sb("rstd", [P, 1])
        idx = sb("idx", [P, TILES, PH * TOPK], U32)
        idc = sb("idc", [P, TOPK], U32)
        gate = sb("gate", [P, TILES, PH * TOPK])
        gate_now = sb("gate_now", [P, TOPK])
        dots = sb("dots", [P, TOPK])
        gel = sb("gel", [P, TOPK])
        coef = sb("coef", [P, TOPK])
        diag = sb("diag", [P, SLOTS, P])
        mix = sb("mix", [P, 8064])
        at = [0]

        def part(words):
            at[0] += words
            assert at[0] <= 8064
            return mix[:, at[0] - words:at[0]]

        rot_c = part(QK)
        rot_s = part(QK)
        rqk = part(QK + HD)
        qkT = part(3 * P)
        qkv = part(AW)
        v_cur = qkv[:, QK:AW]
        v_prev = part(HD)
        k_prev = part(P)
        kA = part(ITERS * P)
        vA = part(ITERS * HD)
        sm = part(GQ * 192)
        prob = part(GQ * 2 * P)
        pT = part(GQ * 2 * P)
        a_on = part(GQ * HD)
        a_oT = part(GQ * HD)
        sink4 = part(GQ)
        mx = part(GQ)
        mxs = part(GQ)
        nm = part(GQ)
        sink_d = part(GQ)
        sink_e = part(GQ)
        den = part(GQ)
        den_s = part(GQ)
        rden = part(GQ)
        at[0] = 0
        sg = part(2 * HALF)
        hq = part(2 * P)
        hk = part(2 * P)
        pre = part(2 * P)
        suf = part(2 * P)
        qb = part(2 * 2 * P)
        kb = part(2 * 2 * P)
        hv = part(2 * P)
        gg = part(2 * P)
        gs = part(2 * P)
        scT = part(2 * P)
        scX = part(2 * P)
        h_on = part(2 * P)
        h_on2 = part(2 * P)
        h_oT = part(2 * P)
        KA = part(8 * P)
        VA = part(8 * P)
        KAc = part(2 * P)
        VAc = part(2 * P)
        lb2 = part(2)
        one_lb2 = part(2)
        hss = part(2)
        hms = part(2)
        him = part(2)
        hrs = part(2)
        rqT = sb("rqT", [P, RHC * P])
        sv = sb("sv", [P, RHC, TOPK])
        si = sb("si", [P, RHC, TOPK], U32)
        sif = sb("sif", [P, RHC, TOPK])
        rest = rqT[:].rearrange("p (c k) -> p c k", k=KEYS)
        cand = sb("cand", [P, RH, TOPK * TOPK])
        crest = sb("crest", [P, RH, TOPK * TOPK])
        ci = sb("ci", [P, RH, TOPK], U32)
        cab = sb("cab", [P, 2, RH, TOPK], U32)
        cabf = sb("cabf", [P, 2, RH, TOPK])
        chosen = sb("chosen", [P, 2, RH, TOPK])
        expert = sb("expert", [P, RH, TOPK])
        cvt = sb("cvt", [P, RH, TOPK])
        cvs = sb("cvs", [P, RH, TOPK])
        ge = sb("ge", [P, RH, TOPK])
        gsum = sb("gsum", [P, RH])
        ginv = sb("ginv", [P, RH])

        acc = ps("acc", [P, D])
        y = ps("y", [P, D])
        rq = y[:, 0:HALF]
        pj = ps("pj", [P, 2, HALF])
        sc = ps("sc", [P, HALF])
        ob = ps("ob", [P, HALF])

        const_in, x0_in = sem("const_in"), sem("x0_in")
        gain_in = [sem("gain_in0"), sem("gain_in1")]
        wattn_in, wattn_out_in = sem("wattn_in"), sem("wattn_out_in")
        whgrn_in = [sem("whgrn_in0"), sem("whgrn_in1")]
        whgrn_out_in = sem("whgrn_out_in")
        wroute_in = sem("wroute_in")
        slot_in = [sem(f"slot_in{k}") for k in range(SLOTS)]
        out_done = sem("out_done")
        dve_done = sem("dve_done")
        passed = {n: sem(f"{n}_passed") for n in ("dve", "pool")}
        h_ready = sem("h_ready")
        ims_ready, rstd_ready, norm_done = sem("ims_ready"), sem("rstd_ready"), sem("norm_done")
        xT_ps, xT_act, xT_dve = sem("xT_ps"), sem("xT_act"), sem("xT_dve")
        lb_zero, lb_exp = sem("lb_zero"), sem("lb_exp")
        cleared = sem("cleared")
        idc_ready, dots_ready, gelu_ready = sem("idc_ready"), sem("dots_ready"), sem("gelu_ready")
        coef_ready, diag_ready, slots_free = sem("coef_ready"), sem("diag_ready"), sem("slots_free")
        a_proj, a_qkv, a_rope, a_qkT_ps, a_qkT = sem("a_proj"), sem("a_qkv"), sem("a_rope"), sem("a_qkT_ps"), sem("a_qkT")
        a_score, a_nm, a_prob, a_sink = sem("a_score"), sem("a_nm"), sem("a_prob"), sem("a_sink")
        a_pT_ps, a_pT_act, a_pT_dve = sem("a_pT_ps"), sem("a_pT_act"), sem("a_pT_dve")
        a_o, a_on_ready, a_oT_ps, a_oT_ready = sem("a_o"), sem("a_on_ready"), sem("a_oT_ps"), sem("a_oT_ready")
        a_outproj = sem("a_outproj")
        h_proj, h_act, h_factors, h_score = sem("h_proj"), sem("h_act"), sem("h_factors"), sem("h_score")
        h_scT, h_o, h_sq, h_ims, h_rstd = sem("h_scT"), sem("h_o"), sem("h_sq"), sem("h_ims"), sem("h_rstd")
        h_on_ready, h_oT_ps, h_oT_ready = sem("h_on_ready"), sem("h_oT_ps"), sem("h_oT_ready")
        h_outproj = sem("h_outproj")
        r_proj, r_qT, r_score, r_done = sem("r_proj"), sem("r_qT"), sem("r_score"), sem("r_done")
        g_shift, g_exp = sem("g_shift"), sem("g_exp")

        CONSTS = ((ident[:], ident_in), (cos_t[:], cos), (sin_t[:], sin), (amask[:], masks_attn),
                  (hmask[:], masks_hgrn), (iota16[:], iota_in.to_broadcast([P, TOPK])),
                  (sink_t[:], sinks.to_broadcast([P, 4 * GQ])), (lbr[:], lb_raw),
                  (ogain[:], out_gain.to_broadcast([P, P])), (h[:, 1], x[1]))
        CONST_BYTES_IN = 16 * len(CONSTS)

        PHASES = [(-1, 0, 0), (0, 0, 1), (1, 1, 0), (2, 1, 1)]
        OWN = ITERS - 1

        def hold(engine, name, semaphore, value):
            engine.wait_ge(semaphore, value)
            engine.sem_inc(passed[name], 1)

        def h_count(phase):
            return 0 if phase < 0 else 2 * phase + 1

        def attn_bank(phase):
            return acc[:, 0:HALF] if phase < 0 else pj[:, 0]

        def bands(ap, n):
            return ap.rearrange("p (n w) -> p n w", n=n)

        def window(tile):
            return (128, amask[:, 0:128]) if tile == 0 else (192, amask[:, 128:320])

        block = ctx.enter_context(nc.Block())

        @block.sync
        def _(sp):
            def load_mixer(layer, tile, i, first):
                n = tile * ITERS + i
                if layer == 0:
                    if not first:
                        sp.wait_ge(a_proj, n)
                    sp.dma_start(wmix[:, 0, 0:KT * AW], attn_in[bass.ds(i, 1)].squeeze(0)).then_inc(wattn_in, 16)
                    if not first:
                        sp.wait_ge(a_outproj, n)
                    sp.dma_start(wmix[:, 1, 0:2 * D], attn_out[bass.ds(i, 1)].squeeze(0)).then_inc(wattn_out_in, 16)
                    return
                for j in range(HH):
                    if first:
                        sp.wait_ge(a_proj, TILES * ITERS)
                        sp.wait_ge(a_outproj, TILES * ITERS)
                    else:
                        sp.wait_ge(h_proj, n * 2 - 1 + j)
                    sp.dma_start(wmix[:, j, 0:KT * HALF], hgrn_in[bass.ds(i * 2 + j, 1)].squeeze(0)).then_inc(whgrn_in[j], 16)
                if not first:
                    sp.wait_ge(h_outproj, n)
                sp.dma_start(wmix[:, :, KT * HALF:5 * D], hgrn_out[bass.ds(i, 1)].squeeze(0)).then_inc(whgrn_out_in, 16)

            def load_route(layer, tile, i, first=False):
                n = (layer * TILES + tile) * ITERS + i
                if not first:
                    sp.wait_ge(r_score, n)
                sp.dma_start(wroute[:], route_w[bass.ds(layer * ITERS + i, 1)].squeeze(0)).then_inc(wroute_in, 16)

            def load_gain(n):
                if n >= 2:
                    sp.wait_ge(norm_done, n - 1)
                row = (0, 2, 0, 2, 1, 3, 1, 3, 4, 4)[n]
                sp.dma_start(gain[:, n % 2], gains[row:row + 1].to_broadcast([P, D])).then_inc(gain_in[n % 2], 16)

            sp.dma_start(h[:, 0], x[0]).then_inc(x0_in, 16)
            load_gain(0)
            for to, of in CONSTS:
                sp.dma_start(to, of).then_inc(const_in, 16)
            load_mixer(0, 0, 0, True)
            load_gain(1)
            for phase, layer, tile in PHASES:
                load_route(layer, tile, 0, first=phase < 0)
                with sp.Fori(1, ITERS) as i:
                    load_mixer(layer, tile, i, False)
                mix_norm = 2 * (phase + 1)
                load_gain(mix_norm + 2)
                if phase < 2:
                    load_mixer(*PHASES[phase + 2][1:], 0, phase == 0)
                load_gain(mix_norm + 3)
                with sp.Fori(1, ITERS) as i:
                    load_route(layer, tile, i)
            for tile in range(TILES):
                sp.wait_ge(norm_done, 9 + tile)
                sp.dma_start(out[tile], xn[:, tile]).then_inc(out_done, 16)
            sp.wait_ge(out_done, 16 * TILES)

        @block.gpsimd
        def _(pool):
            for phase, layer, tile in PHASES:
                with pool.Fori(0, PH) as i:
                    g = (phase + 1) * PH + i
                    hold(pool, "pool", r_done, g + 1)
                    for part_ in range(2):
                        cols = slice(part_ * SLOTS, (part_ + 1) * SLOTS)
                        pool.tensor_copy(idc[:, cols], idx[:, tile, bass.ds(i * TOPK + part_ * SLOTS, SLOTS)]).then_inc(idc_ready, 1)
                        hold(pool, "pool", idc_ready, g * 2 + part_ + 1)
                        for k in range(SLOTS):
                            col = part_ * SLOTS + k
                            hold(pool, "pool", slots_free, g * TOPK + col + 1)
                            pool.indirect_dma_start(
                                out=ring[:, k, :], out_offset=None, in_=experts,
                                in_offset=bass.IndirectOffsetOnAxis(ap=idc[:, col:col + 1], axis=0),
                            ).then_inc(slot_in[k], 16)

        @block.scalar
        def _(act):
            def copy(to, of):
                return act.activation(to, of, ACT.Copy)

            def norm(n, transposed):
                act.wait_ge(ims_ready, n + 1)
                act.activation(rstd[:], ims[:], ACT.Sqrt).then_inc(rstd_ready, 1)
                if transposed:
                    act.wait_ge(xT_ps, n + 1)
                    copy(xTs[:, n % 2, 0:4], pj[:, 0].rearrange("p (k t) -> p k t", k=4)).then_inc(xT_act, 1)

            def attention(tile, i, s):
                n = tile * ITERS + i
                if s == 0:
                    act.wait_ge(a_proj, n + 1)
                    bank = attn_bank(tile - 1)
                    if tile == 0:
                        copy(vA[:, bass.ds(i * HD, HD)], bank[:, QK:AW])
                    else:
                        copy(v_prev, vA[:, bass.ds(i * HD, HD)])
                        copy(k_prev, kA[:, bass.ds(i * P, P)])
                    copy(qkv, bank[:, 0:AW]).then_inc(a_qkv, 1)
                elif s == 1:
                    act.wait_ge(a_qkT_ps, n + 1)
                    if tile == 0:
                        copy(kA[:, bass.ds(i * P, P)], ob[:, 2 * P:3 * P])
                    copy(qkT, ob[:, 0:3 * P]).then_inc(a_qkT, 1)
                elif s == 2:
                    act.wait_ge(a_nm, n + 1)
                    w, _ = window(tile)
                    for g in range(GQ):
                        act.activation(bands(prob, GQ)[:, g, 2 * P - w:2 * P], bands(sm, GQ)[:, g, 0:w], ACT.Exp,
                                       bias=nm[:, g:g + 1], accum_out=den[:, g:g + 1]).then_inc(a_prob, 1)
                    act.activation(sink_e, sink_d, ACT.Exp).then_inc(a_sink, 1)
                elif s == 3:
                    act.wait_ge(a_pT_ps, n + 1)
                    copy(pT[:, 0:HALF], pj[:, 0]).then_inc(a_pT_act, 1)
                elif s == 5:
                    act.wait_ge(a_oT_ps, n + 1)
                    copy(a_oT, sc[:, 256:512]).then_inc(a_oT_ready, 1)

            def hgrn(tile, i, s):
                n = tile * ITERS + i
                if s == 0:
                    act.wait_ge(h_proj, 2 * n + 2)
                    copy(bands(hv, 2), pj[:, :, 256:384])
                    if tile == 0:
                        copy(bands(VA[:, bass.ds(i * 2 * P, 2 * P)], 2), pj[:, :, 256:384])
                    else:
                        copy(KAc, KA[:, bass.ds(i * 2 * P, 2 * P)])
                        copy(VAc, VA[:, bass.ds(i * 2 * P, 2 * P)])
                    act.activation(bands(sg, 2), pj[:, :, :], ACT.Sigmoid).then_inc(h_act, 1)
                elif s == 4:
                    act.wait_ge(h_o, n + 1)
                    for j in range(HH):
                        act.activation(h_on[:, j * P:(j + 1) * P], ob[:, j * P:(j + 1) * P], ACT.Square,
                                       accum_out=hss[:, j:j + 1]).then_inc(h_sq, 1)
                    act.wait_ge(h_ims, n + 1)
                    act.activation(hrs, him, ACT.Sqrt).then_inc(h_rstd, 1)
                elif s == 5:
                    act.wait_ge(h_oT_ps, n + 1)
                    copy(h_oT, ob[:, 256:512]).then_inc(h_oT_ready, 1)

            def routing(n, s):
                if s == 1:
                    act.wait_ge(r_proj, n + 1)
                    copy(rqT[:], rq).then_inc(r_qT, 1)
                elif s == 6:
                    act.wait_ge(g_shift, n + 1)
                    act.activation(ge[:], cvs[:], ACT.Exp).then_inc(g_exp, 1)

            def step(g, s, beside, beside_last=False):
                if g is not None:
                    act.wait_ge(dots_ready, g * STEPS + s + 1)
                    act.activation(gel[:, s * SUB:(s + 1) * SUB], dots[:, s * SUB:(s + 1) * SUB], ACT.Gelu).then_inc(gelu_ready, 1)
                if not beside_last:
                    beside()
                if g is not None:
                    act.wait_ge(coef_ready, g * STEPS + s + 1)
                    for k in range(s * SUB, (s + 1) * SUB):
                        last = act.activation(diag[:, k % SLOTS], ident[:], ACT.Copy, scale=coef[:, k:k + 1])
                    last.then_inc(diag_ready, 1)
                if beside_last:
                    beside()

            norm(0, True)
            act.wait_ge(lb_zero, 1)
            act.activation(lbe[:], lbp[:], ACT.Exp).then_inc(lb_exp, 1)
            for phase, layer, tile in PHASES:
                if phase < 0:
                    def first_half(i):
                        for s in (1, 2, 3):
                            attention(0, i, s)

                    attention(0, 0, 0)
                    with act.Fori(0, ITERS - 1) as i:
                        first_half(i)
                        act.wait_ge(a_o, i + 1)
                        attention(0, i + 1, 0)
                        attention(0, i, 5)
                    first_half(ITERS - 1)
                    attention(0, ITERS - 1, 5)
                else:
                    with act.Fori(0, ITERS) as i:
                        for s in range(STEPS):
                            step(phase * PH + OWN + i, s, lambda: (attention, hgrn)[layer](tile, i, s))
                norm(2 * (phase + 1) + 1, True)
                for s in range(STEPS):
                    step(phase * PH + PH - 1 if phase >= 0 else None, s, lambda: routing((phase + 1) * ITERS, s), s > 2)
                norm(2 * (phase + 2), phase < 2)
                with act.Fori(1, ITERS) as i:
                    for s in range(STEPS):
                        step((phase + 1) * PH + i - 1, s, lambda: routing((phase + 1) * ITERS + i, s), s > 2)
            with act.Fori(OWN, PH) as i:
                for s in range(STEPS):
                    step(3 * PH + i, s, lambda: None)
            norm(9, False)

        @block.vector
        def _(dve):
            link = InOrder(dve, dve_done)

            def norm(n, tile, transposed):
                dve.wait_ge(gain_in[n % 2], 16 * (n // 2 + 1))
                link(dve.tensor_tensor_reduce(out=xn[:, tile], in0=h[:, tile], in1=h[:, tile], scale=1.0, scalar=0.0,
                                              op0=ALU.mult, op1=ALU.add, accum_out=ss[:]))
                link(dve.tensor_scalar(ms[:], ss[:], 1.0 / D, EPS, ALU.mult, ALU.add))
                dve.reciprocal(ims[:], ms[:]).then_inc(ims_ready, 1)
                dve.wait_ge(rstd_ready, n + 1)
                dve.scalar_tensor_tensor(xn[:, tile], h[:, tile], rstd[:], gain[:, n % 2], ALU.mult, ALU.mult).then_inc(norm_done, 1)
                if transposed:
                    dve.wait_ge(xT_ps, n + 1)
                    dve.tensor_copy(xTs[:, n % 2, 4:8], pj[:, 1].rearrange("p (k t) -> p k t", k=4)).then_inc(xT_dve, 1)

            def attention(tile, i, s):
                n = tile * ITERS + i
                w, mask = window(tile)
                if s == 0:
                    hold(dve, "dve", a_qkv, n + 1)
                    dve.tensor_copy(sink4, sink_t[:, bass.ds(i * GQ, GQ)])
                    qk = bands(qkv[:, 0:QK], GQ + 1)
                    heads = [P, GQ + 1, HD // 2]
                    c, sn = cos_t[:, tile].unsqueeze(1), sin_t[:, tile].unsqueeze(1)
                    dve.tensor_tensor(bands(rot_c, GQ + 1), qk, c.broadcast_to([P, GQ + 1, HD]), ALU.mult)
                    dve.tensor_tensor(bands(rot_s, GQ + 1)[:, :, 0:32], qk[:, :, 32:64], sn[:, :, 0:32].broadcast_to(heads), ALU.mult)
                    link(dve.tensor_tensor(bands(rot_s, GQ + 1)[:, :, 32:64], qk[:, :, 0:32], sn[:, :, 32:64].broadcast_to(heads), ALU.mult))
                    dve.tensor_tensor(rqk[:, 0:QK], rot_c, rot_s, ALU.add)
                    dve.tensor_tensor(rqk[:, QK:QK + HD], rot_c[:, QK - HD:QK], rot_s[:, QK - HD:QK], ALU.add).then_inc(a_rope, 1)
                elif s == 2:
                    hold(dve, "dve", a_score, n + 1)
                    for half, bank in ((0, pj[:, 1]), (1, sc)):
                        last = dve.scalar_tensor_tensor(
                            bands(sm, GQ)[:, half:GQ:2, 0:w], bank[:, 0:2 * w].rearrange("p (n w) -> p n w", n=2),
                            HD ** -0.5, mask.unsqueeze(1).broadcast_to([P, 2, w]), ALU.mult, ALU.add)
                    link(last)
                    link(dve.reduce_max(mx, bands(sm, GQ)[:, :, 0:w], AX))
                    link(dve.tensor_tensor(mxs, mx, sink4, ALU.max))
                    dve.tensor_tensor(sink_d, sink4, mxs, ALU.subtract)
                    dve.tensor_scalar(nm, mxs, -1.0, None, ALU.mult).then_inc(a_nm, 1)
                elif s == 3:
                    hold(dve, "dve", a_sink, n + 1)
                    link(dve.tensor_tensor(den_s, den, sink_e, ALU.add))
                    link(dve.reciprocal(rden, den_s))
                    hold(dve, "dve", a_pT_ps, n + 1)
                    dve.tensor_copy(pT[:, HALF:D], ob[:]).then_inc(a_pT_dve, 1)
                elif s == 4:
                    hold(dve, "dve", a_o, n + 1)
                    dve.tensor_tensor(bands(a_on, GQ), bands(sc[:, 0:GQ * HD], GQ), rden.unsqueeze(2).broadcast_to([P, GQ, HD]),
                                      ALU.mult).then_inc(a_on_ready, 1)

            def hgrn(tile, i, s):
                n = tile * ITERS + i

                def produce(level):
                    if level == 0:
                        return
                    side = level % 2
                    if level <= LEVELS:
                        dve.tensor_tensor(bands(kb, 2)[:, side], hk, suf, ALU.mult)
                    dve.tensor_tensor(bands(qb, 2)[:, side], hq, pre, ALU.mult).then_inc(h_factors, 1)
                    if level > LEVELS:
                        return
                    hold(dve, "dve", h_factors, level_count(tile, i, level))
                    b = 1 << (level - 1)
                    blocks = 2 * P // (2 * b)
                    pv = pre.rearrange("p (n two b) -> p n two b", two=2, b=b)
                    sv_ = suf.rearrange("p (n two b) -> p n two b", two=2, b=b)
                    link(dve.tensor_tensor(sv_[:, :, 0], sv_[:, :, 0], pv[:, :, 1, b - 1:b].broadcast_to([P, blocks, b]), ALU.mult))
                    link(dve.tensor_tensor(pv[:, :, 1], pv[:, :, 1], pv[:, :, 0, b - 1:b].broadcast_to([P, blocks, b]), ALU.mult))

                def consume(level):
                    hold(dve, "dve", h_score, level_count(tile, i, level))
                    side = (sc, ob)[level % 2][:, 0:2 * P]
                    if level > LEVELS:
                        return dve.tensor_copy(scX, side)
                    return dve.copy_predicated(bands(scT, 2), hmask[:, level].unsqueeze(1).broadcast_to([P, 2, P]), bands(side, 2))

                if s == 0:
                    hold(dve, "dve", h_act, n + 1)
                    dve.tensor_copy(lb2, lb[:, bass.ds(i * 2, 2)])
                    link(dve.tensor_copy(one_lb2, one_lb[:, bass.ds(i * 2, 2)]))
                    for j in range(HH):
                        last = dve.tensor_scalar(pre[:, j * P:(j + 1) * P], sg[:, j * HALF + P:j * HALF + 2 * P], one_lb2[:, j:j + 1],
                                                 lb2[:, j:j + 1], ALU.mult, ALU.add)
                    link(last)
                    dve.tensor_scalar(hk, pre, -1.0, 1.0, ALU.mult, ALU.add)
                    dve.tensor_tensor(bands(hq, 2), pj[:, :, 0:P], bands(sg, 2)[:, :, 0:P], ALU.mult).then_inc(h_factors, 1)
                    hold(dve, "dve", h_factors, level_count(tile, i, 0))
                    link(dve.memset(suf, 1.0))
                    produce(1)
                    link(dve.tensor_tensor(bands(gs, 2), pj[:, :, 384:512], bands(sg, 2)[:, :, 384:512], ALU.mult))
                    dve.tensor_tensor(bands(gg, 2), bands(gs, 2), ogain[:].unsqueeze(1).broadcast_to([P, 2, P]), ALU.mult)
                    link(consume(0))
                elif s in (1, 2, 3):
                    for level in (2 * s, 2 * s + 1):
                        produce(level)
                        link(consume(level - 1))
                elif s == 4:
                    if tile == 1:
                        produce(8)
                        link(consume(7))
                        consume(8).then_inc(h_scT, 1)
                    else:
                        link(dve.tensor_tensor(KA[:, bass.ds(i * 2 * P, 2 * P)], hk, suf, ALU.mult))
                        consume(7).then_inc(h_scT, 1)
                    hold(dve, "dve", h_sq, 2 * n + 2)
                    link(dve.tensor_scalar(hms, hss, 1.0 / P, EPS, ALU.mult, ALU.add))
                    dve.reciprocal(him, hms).then_inc(h_ims, 1)
                elif s == 5:
                    hold(dve, "dve", h_rstd, n + 1)
                    link(dve.tensor_tensor(bands(h_on2, 2), bands(ob[:, 0:256], 2), hrs.unsqueeze(2).broadcast_to([P, 2, P]), ALU.mult))
                    dve.tensor_tensor(h_on, h_on2, gg, ALU.mult).then_inc(h_on_ready, 1)

            def top16(values, indices, source, remaining, rows):
                for r in rows:
                    last = dve.max(values[:, r, 0:8], source[r])
                link(last)
                for r in rows:
                    dve.max_index(indices[:, r, 0:8], values[:, r, 0:8], source[r])
                    last = dve.match_replace(remaining[:, r], values[:, r, 0:8], source[r], LOWEST)
                link(last)
                for r in rows:
                    last = dve.max(values[:, r, 8:16], remaining[:, r])
                link(last)
                for r in rows:
                    last = dve.max_index(indices[:, r, 8:16], values[:, r, 8:16], remaining[:, r])
                link(last)

            def routing(layer, tile, n, i, s):
                scores = [sc[:, c * KEYS:(c + 1) * KEYS] for c in range(RHC)]
                if s == 2:
                    hold(dve, "dve", r_score, n + 1)
                    top16(sv, si, scores, rest, (0, 1))
                elif s == 3:
                    top16(sv, si, scores, rest, (2, 3))
                elif s == 4:
                    dve.tensor_copy(sif[:], si[:])
                    by_half = sv[:].rearrange("p (h c) k -> p h c k", c=2)
                    grid = [P, RH, TOPK, TOPK]
                    link(dve.tensor_tensor(cand[:].rearrange("p h (a b) -> p h a b", b=TOPK),
                                           by_half[:, :, 0].unsqueeze(3).broadcast_to(grid),
                                           by_half[:, :, 1].unsqueeze(2).broadcast_to(grid), ALU.add))
                elif s == 5:
                    top16(cvt, ci, [cand[:, r] for r in range(RH)], crest, range(RH))
                    dve.tensor_tensor(cvs[:], cvt[:], cvt[:, :, 0:1].broadcast_to([P, RH, TOPK]), ALU.subtract).then_inc(g_shift, 1)
                elif s == 6:
                    dve.tensor_scalar(cab[:, 0], ci[:], 4, None, ALU.logical_shift_right)
                    link(dve.tensor_scalar(cab[:, 1], ci[:], TOPK - 1, None, ALU.bitwise_and))
                    link(dve.tensor_copy(cabf[:], cab[:]))
                    grid = [P, RH, TOPK, TOPK]
                    picks = [a[:].rearrange("p h (k a) -> p h k a", a=TOPK) for a in (cand, crest)]
                    for c in range(2):
                        last = dve.tensor_tensor(picks[c], cabf[:, c].unsqueeze(3).broadcast_to(grid),
                                                 iota16[:].unsqueeze(1).unsqueeze(1).broadcast_to(grid), ALU.is_equal)
                    link(last)
                    for c in range(2):
                        of_half = sif[:].rearrange("p (h c) k -> p h c k", c=2)[:, :, c]
                        last = dve.tensor_tensor(picks[c], picks[c], of_half.unsqueeze(2).broadcast_to(grid), ALU.mult)
                    link(last)
                    for c in range(2):
                        last = dve.reduce_sum(chosen[:, c], picks[c], AX)
                    link(last)
                    link(dve.scalar_tensor_tensor(expert[:], chosen[:, 0], float(KEYS), chosen[:, 1], ALU.mult, ALU.add))
                    here = bass.ds(i * RH * TOPK, RH * TOPK)
                    dve.tensor_scalar(idx[:, tile, here], expert[:].rearrange("p h k -> p (h k)"), float(layer * EXPERTS), None,
                                      ALU.add).then_inc(r_done, RH)
                    hold(dve, "dve", r_done, RH * (n + 1))
                elif s == 7:
                    hold(dve, "dve", g_exp, n + 1)
                    link(dve.reduce_sum(gsum[:], ge[:], AX))
                    link(dve.reciprocal(ginv[:], gsum[:]))
                    link(dve.tensor_tensor(gate[:, tile, bass.ds(i * RH * TOPK, RH * TOPK)].rearrange("p (h k) -> p h k", k=TOPK),
                                           ge[:], ginv[:].unsqueeze(2).broadcast_to([P, RH, TOPK]), ALU.mult))

            def gather_head(tile, i):
                link(dve.tensor_copy(gate_now[:], gate[:, tile, bass.ds(i * TOPK, TOPK)]))

            def step(g, tile, s, beside, beside_last=False):
                if g is not None:
                    for k in range(s * SUB, (s + 1) * SUB):
                        slot = k % SLOTS
                        hold(dve, "dve", slot_in[slot], (g * 2 + k // SLOTS + 1) * 16)
                        last = dve.tensor_tensor_reduce(out=ring[:, slot, 0:D], in0=ring[:, slot, 0:D], in1=xn[:, tile], scale=1.0,
                                                        scalar=0.0, op0=ALU.mult, op1=ALU.add, accum_out=dots[:, k:k + 1])
                    last.then_inc(dots_ready, 1)
                if not beside_last:
                    beside()
                if g is not None:
                    cols = slice(s * SUB, (s + 1) * SUB)
                    hold(dve, "dve", gelu_ready, g * STEPS + s + 1)
                    dve.tensor_tensor(coef[:, cols], gel[:, cols], gate_now[:, cols], ALU.mult).then_inc(coef_ready, 1)
                    if s == STEPS - 1:
                        hold(dve, "dve", coef_ready, (g + 1) * STEPS)
                if beside_last:
                    beside()

            def layer_done(phase, tile):
                dve.wait_ge(slots_free, (phase + 1) * PH * TOPK + SLOTS)
                dve.tensor_copy(h[:, tile], acc[:]).then_inc(h_ready, 1)
                dve.wait_ge(h_ready, h_count(phase) + (2 if phase < 3 else 1))

            dve.memset(prob, 0.0).then_inc(cleared, 1)
            dve.wait_ge(x0_in, 16)
            norm(0, 0, True)
            dve.wait_ge(const_in, CONST_BYTES_IN)
            dve.tensor_tensor(lbp[:], lbr[:], lbr[:], ALU.subtract).then_inc(lb_zero, 1)
            dve.wait_ge(lb_exp, 1)
            link(dve.reciprocal(lbp[:], lbe[:]))
            link(dve.tensor_tensor(lbe[:], lbe[:], lbp[:], ALU.mult))
            link(dve.tensor_tensor(lb[:], lbe[:], lbe[:], ALU.subtract))
            link(dve.tensor_scalar(one_lb[:], lb[:], -1.0, 1.0, ALU.mult, ALU.add))
            for phase, layer, tile in PHASES:
                if phase == 1:
                    link(dve.memset(scT, 0.0))
                if phase < 0:
                    attention(0, 0, 0)
                    with dve.Fori(0, ITERS - 1) as i:
                        link.restart()
                        for s in (2, 3, 4):
                            attention(0, i, s)
                        attention(0, i + 1, 0)
                    for s in (2, 3, 4):
                        attention(0, ITERS - 1, s)
                else:
                    with dve.Fori(0, ITERS) as i:
                        link.restart()
                        gather_head(1 - tile, OWN + i)
                        for s in range(STEPS):
                            step(phase * PH + OWN + i, 1 - tile, s, lambda: (attention, hgrn)[layer](tile, i, s))
                dve.wait_ge((a_outproj, h_outproj)[layer], (tile + 1) * ITERS)
                dve.tensor_copy(h[:, tile], y[:]).then_inc(h_ready, 1)
                dve.wait_ge(h_ready, h_count(phase) + 1)
                norm(2 * (phase + 1) + 1, tile, True)
                if phase >= 0:
                    gather_head(1 - tile, PH - 1)
                for s in range(STEPS):
                    step(phase * PH + PH - 1 if phase >= 0 else None, 1 - tile, s,
                         lambda: routing(layer, tile, (phase + 1) * ITERS, 0, s), s > 2)
                if phase >= 0:
                    layer_done(phase, 1 - tile)
                norm(2 * (phase + 2), 1 - tile, phase < 2)
                with dve.Fori(1, ITERS) as i:
                    link.restart()
                    gather_head(tile, i - 1)
                    for s in range(STEPS):
                        step((phase + 1) * PH + i - 1, tile, s, lambda: routing(layer, tile, (phase + 1) * ITERS + i, i, s), s > 2)
            with dve.Fori(OWN, PH) as i:
                link.restart()
                gather_head(1, i)
                for s in range(STEPS):
                    step(3 * PH + i, 1, s, lambda: None)
            layer_done(3, 1)
            norm(9, 1, False)

        @block.tensor
        def _(pe):
            def norm(n, tile):
                pe.wait_ge(norm_done, n + 1)
                for k in range(KT):
                    last = nc.tensor.transpose(pj[:, k // 4, k % 4 * P:k % 4 * P + P], xn[:, tile, k * P:(k + 1) * P], ident[:])
                last.then_inc(xT_ps, 1)
                pe.wait_ge(xT_act, n + 1)
                pe.wait_ge(xT_dve, n + 1)

            def residual(bank, tile):
                for j in range(2):
                    last = nc.tensor.matmul(bank[:, j * HALF:(j + 1) * HALF], ident[:], h[:, tile, j * HALF:(j + 1) * HALF], start=True, stop=True)
                return last

            def attention(tile, i, s, row_):
                n = tile * ITERS + i
                w, _ = window(tile)
                if s != 6:
                    row_(0)
                if s == 0:
                    pe.wait_ge(wattn_in, 16 * (n + 1))
                    for k in range(KT):
                        last = nc.tensor.matmul(attn_bank(tile - 1)[:, 0:AW], xT[:, k], wmix[:, 0, k * AW:(k + 1) * AW], start=k == 0, stop=k == KT - 1)
                    last.then_inc(a_proj, 1)
                elif s == 1:
                    pe.wait_ge(a_rope, n + 1)
                    for c in range(3):
                        last = nc.tensor.transpose(ob[:, c * P:(c + 1) * P], rqk[:, c * P:(c + 1) * P], ident[:])
                    last.then_inc(a_qkT_ps, 1)
                elif s == 2:
                    pe.wait_ge(a_qkT, n + 1)
                    for g in range(GQ):
                        bank = (pj[:, 1], sc)[g % 2]
                        rows = slice(g % 2 * HD, g % 2 * HD + HD)
                        q = qkT[rows, g // 2 * P:(g // 2 + 1) * P]
                        at_ = g // 2 * w
                        if tile == 1:
                            nc.tensor.matmul(bank[:, at_:at_ + CHUNK], q, k_prev[rows, CHUNK:P], start=True, stop=True)
                        last = nc.tensor.matmul(bank[:, at_ + w - P:at_ + w], q, qkT[rows, 2 * P:3 * P], start=True, stop=True)
                    last.then_inc(a_score, 1)
                elif s == 3:
                    pe.wait_ge(a_prob, GQ * (n + 1))
                    for g in range(GQ):
                        bank = pj[:, 0] if g < 2 else ob
                        for b in range(2):
                            to = (g % 2 * 2 + b) * P
                            last = nc.tensor.transpose(bank[:, to:to + P], prob[:, (g * 2 + b) * P:(g * 2 + b + 1) * P], ident[:])
                    last.then_inc(a_pT_ps, 1)
                elif s == 4:
                    pe.wait_ge(a_pT_act, n + 1)
                    pe.wait_ge(a_pT_dve, n + 1)
                    for g in range(GQ):
                        to = sc[:, g * HD:(g + 1) * HD]
                        if tile == 1:
                            nc.tensor.matmul(to, pT[:, g * 2 * P:(g * 2 + 1) * P], v_prev, start=True, stop=False)
                        last = nc.tensor.matmul(to, pT[:, (g * 2 + 1) * P:(g * 2 + 2) * P], v_cur, start=tile == 0, stop=True)
                    last.then_inc(a_o, 1)
                elif s == 5:
                    pe.wait_ge(a_on_ready, n + 1)
                    for c in range(2):
                        last = nc.tensor.transpose(sc[:, 256 + c * P:256 + (c + 1) * P], a_on[:, c * P:(c + 1) * P], ident[:])
                    last.then_inc(a_oT_ps, 1)
                elif s == 6:
                    pe.wait_ge(a_oT_ready, n + 1)
                    pe.wait_ge(wattn_out_in, 16 * (n + 1))
                    for c in range(2):
                        for j in range(2):
                            last = nc.tensor.matmul(y[:, j * HALF:(j + 1) * HALF], a_oT[:, c * P:(c + 1) * P],
                                                    wmix[:, 1, c * D + j * HALF:c * D + (j + 1) * HALF], start=False, stop=True,
                                                    skip_group_check=True)
                        if c == 0:
                            row_(0)
                    last.then_inc(a_outproj, 1)
                row_(1)

            def project(n, j, part_):
                w = wmix[:, j, 0:KT * HALF].rearrange("p (k c) -> p k c", k=KT)
                if part_ == 0:
                    pe.wait_ge(whgrn_in[j], 16 * (n + 1))
                    for c in range(2):
                        for k in range(KT):
                            nc.tensor.matmul(pj[:, j, c * P:(c + 1) * P], w[:, k, c * P:(c + 1) * P], xT[:, k], start=k == 0, stop=k == KT - 1)
                else:
                    for k in range(KT):
                        last = nc.tensor.matmul(pj[:, j, 256:512], xT[:, k], w[:, k, 256:512], start=k == 0, stop=k == KT - 1)
                    last.then_inc(h_proj, 1)

            def hgrn(tile, i, s, row_, ahead):
                n = tile * ITERS + i

                def scores(level):
                    pe.wait_ge(h_factors, level_count(tile, i, level))
                    bank = (sc, ob)[level % 2]
                    side = level % 2 * 256
                    for j in range(HH):
                        cols = slice(side + j * P, side + (j + 1) * P)
                        own = slice(j * P, (j + 1) * P)
                        keys = hk[:, own] if level == 0 else KAc[:, own] if level > LEVELS else kb[:, cols]
                        last = nc.tensor.matmul(bank[:, own], keys, hq[:, own] if level == 0 else qb[:, cols], start=True, stop=True)
                    last.then_inc(h_score, 1)

                if s < 4:
                    scores(2 * s)
                    row_(0)
                    scores(2 * s + 1)
                    row_(1)
                elif s == 4:
                    if tile == 1:
                        scores(8)
                    row_(0)
                    pe.wait_ge(h_scT, n + 1)
                    for j in range(HH):
                        own = slice(j * P, (j + 1) * P)
                        last = nc.tensor.matmul(ob[:, own], scT[:, own], hv[:, own], start=True, stop=tile == 0)
                        if tile == 1:
                            last = nc.tensor.matmul(ob[:, own], scX[:, own], VAc[:, own], start=False, stop=True)
                    last.then_inc(h_o, 1)
                    row_(1)
                elif s == 5:
                    pe.wait_ge(h_on_ready, n + 1)
                    for j in range(HH):
                        last = nc.tensor.transpose(ob[:, 256 + j * P:256 + (j + 1) * P], h_on[:, j * P:(j + 1) * P], ident[:])
                    last.then_inc(h_oT_ps, 1)
                    row_(0)
                    pe.wait_ge(h_oT_ready, n + 1)
                    pe.wait_ge(whgrn_out_in, 16 * (n + 1))
                    for c in range(HH):
                        for j in range(2):
                            last = nc.tensor.matmul(y[:, j * HALF:(j + 1) * HALF], h_oT[:, c * P:(c + 1) * P],
                                                    wmix[:, c, KT * HALF + j * HALF:KT * HALF + (j + 1) * HALF], start=False, stop=True,
                                                    skip_group_check=True)
                    last.then_inc(h_outproj, 1)
                    row_(1)
                else:
                    row_(0)
                    row_(1)
                if ahead and s in (3, 4, 6, 7):
                    project(n + 1, *{3: (0, 0), 4: (0, 1), 6: (1, 0), 7: (1, 1)}[s])

            def routing(n, s):
                if s < 2:
                    if s == 0:
                        pe.wait_ge(wroute_in, 16 * (n + 1))
                    for c in (2 * s, 2 * s + 1):
                        for k in range(KT):
                            last = nc.tensor.matmul(rq[:, c * P:(c + 1) * P], wroute[:, (k * RHC + c) * P:(k * RHC + c + 1) * P], xT_route[:, k],
                                                    start=k == 0, stop=k == KT - 1)
                    if s == 1:
                        last.then_inc(r_proj, 1)
                elif s == 2:
                    pe.wait_ge(r_qT, n + 1)
                    for c in range(RHC):
                        last = nc.tensor.matmul(sc[:, c * KEYS:(c + 1) * KEYS], rqT[:, c * P:(c + 1) * P],
                                                wroute[:, (KT * RHC + c) * P:(KT * RHC + c + 1) * P], start=True, stop=True)
                    last.then_inc(r_score, 1)
                elif s == 7:
                    pe.wait_ge(r_done, RH * (n + 1))

            def row(g, k):
                if k % SUB == 0:
                    pe.wait_ge(diag_ready, g * STEPS + k // SUB + 1)
                slot = k % SLOTS
                for j in range(2):
                    last = nc.tensor.matmul(acc[:, j * HALF:(j + 1) * HALF], diag[:, slot], ring[:, slot, D + j * HALF:D + (j + 1) * HALF],
                                            start=False, stop=True, skip_group_check=True)
                last.then_inc(slots_free, 1)

            def beside_rows(g, mixer, behind):
                for s in range(STEPS):
                    mixer(s, (lambda k: row(g, (s - 1) * SUB + k)) if s >= behind else (lambda k: None))
                    if s < behind - 1:
                        row(g, s * SUB)
                        row(g, s * SUB + 1)
                row(g, TOPK - 2)
                row(g, TOPK - 1)

            pe.wait_ge(x0_in, 16)
            pe.wait_ge(const_in, CONST_BYTES_IN)
            pe.wait_ge(cleared, 1)
            for phase, layer, tile in PHASES:
                if phase >= 0:
                    pe.wait_ge(h_ready, h_count(phase))
                last = residual(y, tile)
                if phase < 0:
                    last.then_inc(slots_free, SLOTS)
                    norm(0, tile)
                    def alone(i, steps):
                        for s in steps:
                            attention(0, i, s, lambda k: None)

                    alone(0, (0,))
                    with pe.Fori(0, ITERS - 1) as i:
                        alone(i, (1, 2, 3))
                        alone(i + 1, (0,))
                        alone(i, (4, 5, 6, 7))
                    alone(ITERS - 1, range(1, STEPS))
                elif layer == 0:
                    with pe.Fori(0, ITERS) as i:
                        beside_rows(phase * PH + OWN + i, lambda s, row_: attention(tile, i, s, row_), 2)
                else:
                    with pe.Fori(0, ITERS - 1) as i:
                        beside_rows(phase * PH + OWN + i, lambda s, row_: hgrn(tile, i, s, row_, True), 1)
                    beside_rows(phase * PH + PH - 2, lambda s, row_: hgrn(tile, ITERS - 1, s, row_, False), 1)
                norm(2 * (phase + 1) + 1, tile)
                for s in range(STEPS):
                    routing((phase + 1) * ITERS, s)
                    if phase >= 0:
                        row(phase * PH + PH - 1, s * SUB)
                        row(phase * PH + PH - 1, s * SUB + 1)
                pe.wait_ge(h_ready, h_count(phase + 1))
                residual(acc, tile)
                if phase < 2:
                    norm(2 * (phase + 2), 1 - tile)

                def route_beside_rows(i, ahead):
                    for s in range(STEPS):
                        routing((phase + 1) * ITERS + i, s)
                        for k in range(SUB):
                            row((phase + 1) * PH + i - 1, s * SUB + k)
                        if ahead and 3 <= s < 7:
                            project((1 - tile) * ITERS, (s - 3) // 2, (s - 3) % 2)

                with pe.Fori(1, ITERS - 1) as i:
                    route_beside_rows(i, False)
                route_beside_rows(ITERS - 1, phase in (0, 1))
            with pe.Fori(OWN, PH) as i:
                for k in range(TOPK):
                    row(3 * PH + i, k)


def shape_constants():
    pos = np.arange(TILES * P, dtype=np.float32)[:, None]
    freq = np.float32(10000.0) ** (-np.arange(0, HD, 2, dtype=np.float32) / np.float32(HD))
    angle = (pos * freq[None]).astype(np.float32)
    c, s = np.cos(angle), np.sin(angle)
    cos = np.concatenate([c, c], 1).reshape(TILES, P, HD).transpose(1, 0, 2)
    sin = np.concatenate([-s, s], 1).reshape(TILES, P, HD).transpose(1, 0, 2)
    attn = np.zeros((P, 320), np.float32)
    attn[:CHUNK, CHUNK:128] = BLOCKED
    attn[:CHUNK, 128 + 128:] = BLOCKED
    attn[CHUNK:, 128:128 + CHUNK] = BLOCKED
    s_, t_ = np.arange(P)[:, None], np.arange(P)[None, :]
    hgrn = [s_ == t_]
    for level in range(LEVELS):
        b = 1 << level
        hgrn.append((s_ // (2 * b) == t_ // (2 * b)) & (s_ % (2 * b) < b) & (t_ % (2 * b) >= b))
    return {
        "cos": np.ascontiguousarray(cos, np.float32), "sin": np.ascontiguousarray(sin, np.float32),
        "masks_attn": attn, "masks_hgrn": np.ascontiguousarray(np.stack(hgrn, 1).astype(np.uint32)),
        "ident_in": np.eye(P, dtype=np.float32), "iota_in": np.arange(TOPK, dtype=np.float32)[None],
    }


def lay_out(a):
    def rows_by_partition(w):
        return w.reshape(-1, P, w.shape[-1]).transpose(1, 0, 2)

    w = a["attn_w_in"][0]
    q, k, v = w[:, :1024], w[:, 1024:1280], w[:, 1280:]
    attn_in = np.stack([rows_by_partition(np.concatenate(
        [q[:, g * 256:(g + 1) * 256], k[:, g * 64:(g + 1) * 64], v[:, g * 64:(g + 1) * 64]], 1)).reshape(P, -1) for g in range(4)])
    attn_out = a["attn_w_out"][0].reshape(4, 2, P, D).transpose(0, 2, 1, 3).reshape(4, P, 2 * D)
    w = a["hgrn_w_in"][0].reshape(KT, P, 4, 8, P)
    hgrn_in = w.transpose(3, 1, 0, 2, 4).reshape(8, P, KT * HALF)
    hgrn_out = a["hgrn_w_out"][0].reshape(4, HH, P, D).transpose(0, 2, 1, 3)
    wq = a["peer_w_q"].reshape(2, KT, P, ITERS, RHC, P).transpose(0, 3, 2, 1, 4, 5).reshape(2 * ITERS, P, -1)
    keys = a["peer_sub_keys"].reshape(2, ITERS, RHC, KEYS, P).transpose(0, 1, 4, 2, 3).reshape(2 * ITERS, P, -1)
    return {
        "x": a["x"].reshape(TILES, P, D),
        "gains": np.concatenate([a["mixer_norm"], a["ffn_norm"], a["final_norm"][None]]),
        "sinks": a["attn_sinks"], "lb_raw": a["hgrn_lb_raw"][0].reshape(8, P).T, "out_gain": a["hgrn_out_norm"],
        "attn_in": attn_in, "attn_out": attn_out, "hgrn_in": hgrn_in, "hgrn_out": hgrn_out,
        "route_w": np.concatenate([wq, keys], 2),
        "experts": np.concatenate([a["peer_u"], a["peer_v"]], 2).reshape(2 * EXPERTS, 2 * D),
    }


_ORDER = ["x", "cos", "sin", "masks_attn", "masks_hgrn", "ident_in", "iota_in", "gains", "sinks", "lb_raw", "out_gain",
          "attn_in", "attn_out", "hgrn_in", "hgrn_out", "route_w", "experts"]


def kernel(**inputs):
    import concourse.bacc as bacc
    from concourse.bass_utils import run_bass_kernel_spmd

    arrays = {**lay_out({n: np.asarray(v) for n, v in inputs.items()}), **shape_constants()}
    arrays = {n: np.ascontiguousarray(v) for n, v in arrays.items()}
    nc = bacc.Bacc("TRN2", target_bir_lowering=False, num_devices=1)
    args = [nc.dram_tensor(n, arrays[n].shape, mybir.dt.from_np(arrays[n].dtype), kind="ExternalInput").ap() for n in _ORDER]
    args.append(nc.dram_tensor("out", (TILES, P, D), F32, kind="ExternalOutput").ap())
    trunk(nc, *args)
    r = run_bass_kernel_spmd(nc, [arrays], core_ids=[0])
    return r.results[0]["out"].reshape(1, TILES * P, D)
```
